# Optimizing a Trainium2 kernel written in Bass

```python
import jax
import jax.numpy as jnp
from jax import lax
import numpy as np

D_MODEL = 1024
BATCH = 1
SEQ = 1024
DEPTH = 1

GRID_W = 64
CTX_LEN = 256
N_MOD = 9
NORM_EPS = 1e-6
D_FF = 2816

NA_HEADS = 8
NA_HEAD_DIM = 64
NA_WIDTH = NA_HEADS * NA_HEAD_DIM
NA_WIN_H = 8
NA_WIN_W = 16
NA_QC = 16
NA_KC = NA_QC + NA_WIN_W

RW_HEADS = 8
RW_HEAD_DIM = 64
RW_WIDTH = RW_HEADS * RW_HEAD_DIM
RW_DECAY_LORA = 64
RW_AAA_LORA = 64
RW_GATE_LORA = 128
RW_GN_EPS = 64e-5

OFF_RW = 3 * NA_WIDTH
RW_SHIFT_COLS = 3 * RW_WIDTH + 2 * RW_DECAY_LORA + 2 * RW_AAA_LORA + RW_GATE_LORA
OFF_GATE = OFF_RW + RW_SHIFT_COLS
IN_COLS = OFF_GATE + 2 * D_MODEL
RW_SPLITS = (RW_WIDTH, 2 * RW_WIDTH, 3 * RW_WIDTH, 3 * RW_WIDTH + 2 * RW_DECAY_LORA, 3 * RW_WIDTH + 2 * RW_DECAY_LORA + 2 * RW_AAA_LORA)

kernel_name = 'hybrid_na_rwkv7_macaron_dit_layer'

def rmsnorm(x, g):
    xf = x.astype(jnp.float32)
    y = xf * lax.rsqrt(jnp.mean(xf * xf, axis=-1, keepdims=True) + NORM_EPS)
    return (y * g.astype(jnp.float32)).astype(x.dtype)

def modulated_norm(x, g, mod, i):
    return rmsnorm(x, g) * (1 + mod[i + 1]) + mod[i]

def swiglu(h, wg, wu, wd):
    return (jax.nn.silu(h @ wg) * (h @ wu)) @ wd

def split_heads(t, h):
    return t.reshape(t.shape[:-1] + (h, t.shape[-1] // h))

def token_shift(f, mu_prev, mu_next):
    prev = jnp.pad(f[:, :-1], ((0, 0), (1, 0), (0, 0)))
    nxt = jnp.pad(f[:, 1:], ((0, 0), (0, 1), (0, 0)))
    return f + mu_prev * (prev - f) + mu_next * (nxt - f)

def na_attention(q, k, v, kc, vc, rpb):
    B, T, H, d = q.shape
    rows = T // GRID_W
    kr = min(NA_WIN_H, rows)
    ncb = GRID_W // NA_QC
    qcol = np.arange(GRID_W).reshape(ncb, NA_QC)
    cb = np.clip(np.arange(ncb) * NA_QC - NA_WIN_W // 2, 0, GRID_W - NA_KC)
    kcol = cb[:, None] + np.arange(NA_KC)
    s = np.clip(qcol - NA_WIN_W // 2, 0, GRID_W - NA_WIN_W)
    valid = (kcol[:, None, :] >= s[..., None]) & (kcol[:, None, :] < s[..., None] + NA_WIN_W)
    valid_full = np.broadcast_to(valid[:, :, None, :], (ncb, NA_QC, kr, NA_KC)).reshape(ncb, NA_QC, kr * NA_KC)
    dc_idx = np.clip(kcol[:, None, :] - qcol[..., None] + NA_WIN_W - 1, 0, 2 * NA_WIN_W - 2)
    scale = d ** -0.5
    kg = k.reshape(B, rows, GRID_W, H, d).transpose(0, 3, 1, 2, 4)
    vg = v.reshape(B, rows, GRID_W, H, d).transpose(0, 3, 1, 2, 4)
    qg = q.reshape(B, rows, ncb, NA_QC, H, d).transpose(1, 0, 4, 2, 3, 5)
    kc_t = kc.transpose(0, 2, 1, 3)
    vc_t = vc.transpose(0, 2, 1, 3)
    n_loc = kr * NA_KC

    def row_fn(args):
        i, q_i = args
        r0 = jnp.clip(i - kr // 2, 0, rows - kr)
        k_r = lax.dynamic_slice_in_dim(kg, r0, kr, axis=2)
        v_r = lax.dynamic_slice_in_dim(vg, r0, kr, axis=2)
        k_b = k_r[:, :, :, kcol].transpose(0, 1, 3, 2, 4, 5).reshape(B, H, ncb, n_loc, d)
        v_b = v_r[:, :, :, kcol].transpose(0, 1, 3, 2, 4, 5).reshape(B, H, ncb, n_loc, d)
        s_loc = jnp.einsum('bhmqd,bhmkd->bhmqk', q_i, k_b).astype(jnp.float32) * scale
        dr = r0 + jnp.arange(kr) - i + (NA_WIN_H - 1)
        bias = rpb[:, dr][:, :, dc_idx]
        bias = bias.transpose(0, 2, 3, 1, 4).reshape(H, ncb, NA_QC, n_loc).astype(jnp.float32)
        s_loc = jnp.where(valid_full, s_loc + bias, -jnp.inf)
        s_ctx = jnp.einsum('bhmqd,bhcd->bhmqc', q_i, kc_t).astype(jnp.float32) * scale
        p = jax.nn.softmax(jnp.concatenate([s_loc, s_ctx], axis=-1), axis=-1).astype(v.dtype)
        return (jnp.einsum('bhmqk,bhmkd->bhmqd', p[..., :n_loc], v_b)
                + jnp.einsum('bhmqc,bhcd->bhmqd', p[..., n_loc:], vc_t))

    o = lax.map(row_fn, (jnp.arange(rows), qg))
    return o.transpose(1, 0, 3, 4, 2, 5).reshape(B, T, H * d)

def context_attention(q, k, v):
    s = jnp.einsum('bqhd,bkhd->bhqk', q, k).astype(jnp.float32) * NA_HEAD_DIM ** -0.5
    p = jax.nn.softmax(s, axis=-1).astype(v.dtype)
    o = jnp.einsum('bhqk,bkhd->bqhd', p, v)
    return o.reshape(o.shape[:2] + (NA_WIDTH,))

def rwkv_prep(f, w0, w_up, a0, a_up, g_up, k_k, k_a):
    B, T, _ = f.shape
    f32 = jnp.float32
    r, k, v, wl, al, gl = jnp.split(f, RW_SPLITS, axis=-1)
    wl = wl.reshape(B, T, 2, RW_DECAY_LORA)
    al = al.reshape(B, T, 2, RW_AAA_LORA)
    w_log = -jax.nn.softplus(-(w0 + jnp.einsum('btdr,drc->btdc', jnp.tanh(wl), w_up)).astype(f32)) - 0.5
    decay = jnp.exp(-jnp.exp(w_log))
    a = jax.nn.sigmoid((a0 + jnp.einsum('btdr,drc->btdc', al, a_up)).astype(f32))
    g = jax.nn.sigmoid(gl) @ g_up
    kk = split_heads((k * k_k).astype(f32), RW_HEADS)
    kk = kk * lax.rsqrt(jnp.maximum(jnp.sum(kk * kk, axis=-1, keepdims=True), 1e-12))
    k_dir = k.astype(f32)[:, :, None, :] * (1 + (a - 1) * k_a.astype(f32))
    return (split_heads(r.astype(f32), RW_HEADS), split_heads(v.astype(f32), RW_HEADS), kk,
            split_heads(decay, RW_HEADS), split_heads(a, RW_HEADS), split_heads(k_dir, RW_HEADS), g)

def rwkv_scan(S0, r, decay, kk, a, k, v, reverse, emit):
    xs = tuple(jnp.swapaxes(t, 0, 1) for t in (r, decay, kk, kk * a, k, v))

    def step(S, inp):
        r_t, w_t, kk_t, b_t, k_t, v_t = inp
        sa = jnp.einsum('bhij,bhj->bhi', S, kk_t)
        S = S * w_t[:, :, None, :] - sa[..., None] * b_t[:, :, None, :] + v_t[..., None] * k_t[:, :, None, :]
        if emit:
            return S, jnp.einsum('bhij,bhj->bhi', S, r_t)
        return S, None

    S, ys = lax.scan(step, S0, xs, reverse=reverse)
    return S, (jnp.swapaxes(ys, 0, 1) if emit else None)

def rwkv_bidir(feats, s_f0, s_b0, emit):
    r, v, kk, decay, a, k_dir, _ = feats
    s_f, y_f = rwkv_scan(s_f0, r, decay[:, :, 0], kk, a[:, :, 0], k_dir[:, :, 0], v, False, emit)
    s_b, y_b = rwkv_scan(s_b0, r, decay[:, :, 1], kk, a[:, :, 1], k_dir[:, :, 1], v, True, emit)
    return s_f, s_b, (y_f + y_b if emit else None)

def rwkv_out(y, feats, r_k, ln_w, ln_b):
    r, v, _, _, _, k_dir, g = feats
    B, T = y.shape[:2]
    mean = jnp.mean(y, axis=-1, keepdims=True)
    var = jnp.mean(jnp.square(y - mean), axis=-1, keepdims=True)
    yn = ((y - mean) * lax.rsqrt(var + RW_GN_EPS)).reshape(B, T, RW_WIDTH) * ln_w + ln_b
    bonus = jnp.sum(r[:, :, None] * k_dir * r_k.astype(jnp.float32), axis=(2, 4))[..., None] * v
    return (yn + bonus.reshape(B, T, RW_WIDTH)) * g

def merge_branches(p, o_na, o_rw, b_gate, p_na, p_rw, w_out):
    gates = jax.nn.sigmoid(p[..., OFF_GATE:] + b_gate)
    g_na, g_rw = jnp.split(gates, 2, axis=-1)
    return (g_na * (o_na @ p_na) + g_rw * (o_rw @ p_rw)) @ w_out

def setup_inputs(seed: int = 0) -> dict:
    key = jax.random.key(seed)
    ks = jax.random.split(key, 40)
    f32 = jnp.float32
    L = DEPTH
    D = D_MODEL

    def nrm(k, shape, s):
        return s * jax.random.normal(k, shape, f32)

    w0_base = -6.0 + 5.0 * jnp.linspace(0.0, 1.0, RW_WIDTH, dtype=f32) ** 1.5
    return {
        'x': nrm(ks[0], (BATCH, SEQ, D), 1.0),
        'c': nrm(ks[1], (BATCH, D), 1.0),
        'ctx': nrm(ks[2], (BATCH, CTX_LEN, D), 1.0),
        'c_ctx': nrm(ks[3], (D,), 1.0),
        'w_ada': nrm(ks[4], (L, D, N_MOD * D), 0.5 * D ** -0.5),
        'b_ada': nrm(ks[5], (L, N_MOD * D), 0.02),
        'norm_ffn1': 1.0 + nrm(ks[6], (L, D), 0.05),
        'norm_mix': 1.0 + nrm(ks[7], (L, D), 0.05),
        'norm_ffn2': 1.0 + nrm(ks[8], (L, D), 0.05),
        'norm_final': 1.0 + nrm(ks[9], (D,), 0.05),
        'ffn1_wg': nrm(ks[10], (L, D, D_FF), D ** -0.5),
        'ffn1_wu': nrm(ks[11], (L, D, D_FF), D ** -0.5),
        'ffn1_wd': nrm(ks[12], (L, D_FF, D), D_FF ** -0.5),
        'ffn2_wg': nrm(ks[13], (L, D, D_FF), D ** -0.5),
        'ffn2_wu': nrm(ks[14], (L, D, D_FF), D ** -0.5),
        'ffn2_wd': nrm(ks[15], (L, D_FF, D), D_FF ** -0.5),
        'w_in': nrm(ks[16], (L, D, IN_COLS), D ** -0.5),
        'b_gate': nrm(ks[17], (L, 2 * D), 0.1),
        'na_rpb': nrm(ks[18], (L, NA_HEADS, 2 * NA_WIN_H - 1, 2 * NA_WIN_W - 1), 0.1),
        'rw_mu': jax.random.uniform(ks[19], (L, 2, RW_SHIFT_COLS), f32, 0.0, 0.5),
        'rw_w0': w0_base + nrm(ks[20], (L, 2, RW_WIDTH), 0.1),
        'rw_w_up': nrm(ks[21], (L, 2, RW_DECAY_LORA, RW_WIDTH), 0.1),
        'rw_a0': nrm(ks[22], (L, 2, RW_WIDTH), 0.1),
        'rw_a_up': nrm(ks[23], (L, 2, RW_AAA_LORA, RW_WIDTH), RW_AAA_LORA ** -0.5),
        'rw_g_up': nrm(ks[24], (L, RW_GATE_LORA, RW_WIDTH), RW_GATE_LORA ** -0.5),
        'rw_k_k': 0.85 + nrm(ks[25], (L, RW_WIDTH), 0.05),
        'rw_k_a': 1.0 + nrm(ks[26], (L, RW_WIDTH), 0.05),
        'rw_r_k': nrm(ks[27], (L, RW_HEADS, RW_HEAD_DIM), 0.1),
        'rw_ln_w': 1.0 + nrm(ks[28], (L, RW_WIDTH), 0.05),
        'rw_ln_b': nrm(ks[29], (L, RW_WIDTH), 0.02),
        'p_na': nrm(ks[30], (L, NA_WIDTH, D), NA_WIDTH ** -0.5),
        'p_rw': nrm(ks[31], (L, RW_WIDTH, D), RW_WIDTH ** -0.5),
        'w_out': nrm(ks[32], (L, D, D), D ** -0.5),
    }

def reference(x, c, ctx, c_ctx, w_ada, b_ada, norm_ffn1, norm_mix, norm_ffn2, norm_final,
              ffn1_wg, ffn1_wu, ffn1_wd, ffn2_wg, ffn2_wu, ffn2_wd, w_in, b_gate, na_rpb,
              rw_mu, rw_w0, rw_w_up, rw_a0, rw_a_up, rw_g_up, rw_k_k, rw_k_a, rw_r_k, rw_ln_w, rw_ln_b,
              p_na, p_rw, w_out):
    B = x.shape[0]
    xc = ctx
    for l in range(DEPTH):
        is_last = l == DEPTH - 1
        mod_x = (jax.nn.silu(c) @ w_ada[l] + b_ada[l]).reshape(B, N_MOD, D_MODEL).transpose(1, 0, 2)[:, :, None, :]
        mod_c = (jax.nn.silu(c_ctx) @ w_ada[l] + b_ada[l]).reshape(N_MOD, D_MODEL)

        x = x + 0.5 * mod_x[2] * swiglu(modulated_norm(x, norm_ffn1[l], mod_x, 0), ffn1_wg[l], ffn1_wu[l], ffn1_wd[l])
        xc = xc + 0.5 * mod_c[2] * swiglu(modulated_norm(xc, norm_ffn1[l], mod_c, 0), ffn1_wg[l], ffn1_wu[l], ffn1_wd[l])

        px = modulated_norm(x, norm_mix[l], mod_x, 3) @ w_in[l]
        pc = modulated_norm(xc, norm_mix[l], mod_c, 3) @ w_in[l]

        qx, kx, vx = [split_heads(t, NA_HEADS) for t in jnp.split(px[..., :OFF_RW], 3, axis=-1)]
        qc, kc, vc = [split_heads(t, NA_HEADS) for t in jnp.split(pc[..., :OFF_RW], 3, axis=-1)]
        o_na = na_attention(qx, kx, vx, kc, vc, na_rpb[l])

        rw_params = (rw_w0[l], rw_w_up[l], rw_a0[l], rw_a_up[l], rw_g_up[l], rw_k_k[l], rw_k_a[l])
        feats_x = rwkv_prep(token_shift(px[..., OFF_RW:OFF_GATE], rw_mu[l, 0], rw_mu[l, 1]), *rw_params)
        feats_c = rwkv_prep(token_shift(pc[..., OFF_RW:OFF_GATE], rw_mu[l, 0], rw_mu[l, 1]), *rw_params)
        s0 = jnp.zeros((B, RW_HEADS, RW_HEAD_DIM, RW_HEAD_DIM), jnp.float32)
        s_cf, s_cb, y_c = rwkv_bidir(feats_c, s0, s0, not is_last)
        _, _, y_x = rwkv_bidir(feats_x, s_cf, s_cb, True)
        o_rw = rwkv_out(y_x, feats_x, rw_r_k[l], rw_ln_w[l], rw_ln_b[l]).astype(x.dtype)

        x = x + mod_x[5] * merge_branches(px, o_na, o_rw, b_gate[l], p_na[l], p_rw[l], w_out[l])
        if not is_last:
            o_na_c = context_attention(qc, kc, vc)
            o_rw_c = rwkv_out(y_c, feats_c, rw_r_k[l], rw_ln_w[l], rw_ln_b[l]).astype(xc.dtype)
            xc = xc + mod_c[5] * merge_branches(pc, o_na_c, o_rw_c, b_gate[l], p_na[l], p_rw[l], w_out[l])
            xc = xc + 0.5 * mod_c[8] * swiglu(modulated_norm(xc, norm_ffn2[l], mod_c, 6), ffn2_wg[l], ffn2_wu[l], ffn2_wd[l])

        x = x + 0.5 * mod_x[8] * swiglu(modulated_norm(x, norm_ffn2[l], mod_x, 6), ffn2_wg[l], ffn2_wu[l], ffn2_wd[l])
    return rmsnorm(x, norm_final)


_drawn_inputs = setup_inputs


def setup_inputs(seed=0):
    import zlib

    import numpy as np

    out = dict(_drawn_inputs(seed))
    spreads = {}
    factors = {'b_ada': 3.706,
     'norm_ffn1': 7.192,
     'norm_mix': 6.31,
     'norm_ffn2': 31.431,
     'b_gate': 8.0,
     'na_rpb': 195.953,
     'rw_w_up': 25.331,
     'rw_a0': 8.0,
     'rw_k_k': 165.704,
     'rw_k_a': 5.019,
     'rw_ln_w': 200.0,
     'rw_ln_b': 200.0,
     'rw_w0': 5.858}
    for name, (base, spread) in spreads.items():
        noise = np.random.default_rng([zlib.crc32(name.encode()), seed]).standard_normal(out[name].shape)
        drawn = base * np.exp(spread * noise) if base else spread * noise
        out[name] = jnp.asarray(drawn.astype(out[name].dtype))
    for name, factor in factors.items():
        out[name] = (out[name] * factor).astype(out[name].dtype)
    return out
```

```python
from contextlib import ExitStack

import numpy as np

import concourse.bass as bass
from concourse import mybir

ALU = mybir.AluOpType
ACT = mybir.ActivationFunctionType
AX = mybir.AxisListType
F32 = mybir.dt.float32
F32R = mybir.dt.float32r
U8 = mybir.dt.uint8

P = 128
D = 1024
KT = D // P
SEQ = 1024
CTX = 256
TOK = SEQ + CTX
D_FF = 2816
FT = D_FF // P
GRID_W = 64
ROWS = SEQ // GRID_W
HEADS = 8
HD = 64
HP = HEADS // 2
WIN_H, WIN_W = 8, 16
RPB_ROW = 2 * GRID_W - 1
NMOD = 9
EPS = 1e-6
GN_EPS = 64e-5
KAPPA = 0.6065306597126334
MASKED = -1e30
RW_TILES = 15
BANK = 512
CH = 128
NCH = TOK // CH
STREAM = CTX + SEQ + CTX

PAR = {}
_at = 0
for _name, _n in (("c", KT), ("c_ctx", KT), ("b_ada", NMOD * KT), ("norm_ffn1", KT), ("norm_mix", KT),
                  ("norm_ffn2", KT), ("norm_final", KT), ("b_gate", 2 * KT), ("mu_prev", RW_TILES),
                  ("mu_next", RW_TILES), ("w0", 2 * HP), ("a0", 2 * HP), ("k_k", HP), ("k_a", HP),
                  ("r_k", HP), ("ln_w", HP), ("ln_b", HP)):
    PAR[_name] = (_at, _n)
    _at += _n
PAR_COLS = _at


class Kept:
    pass


class Chain:

    def __init__(self, eng, sem, at=0):
        self.eng, self.sem, self.at, self.n = eng, sem, at, 0

    def done(self, ins):
        ins.then_inc(self.sem, 1)
        self.n += 1
        return self.n

    def wait(self, n=None):
        self.eng.wait_ge(self.sem, self.at + (self.n if n is None else n))


class Phase(ExitStack):
    last = set()

    def __init__(self, nc, tag):
        super().__init__()
        self.nc, self.tag, self.taken = nc, tag, set()

    def __exit__(self, *raised):
        super().__exit__(*raised)
        start = None
        for n in sorted(self.taken):
            if start is None:
                start = n
            if n + 1 not in self.taken:
                self.nc.gpsimd.sem_clear(range(start, n + 1))
                start = None
        Phase.last = self.taken

    def sb(self, name, shape, dtype=F32):
        return self.enter_context(self.nc.sbuf_tensor(f"{self.tag}_{name}", shape, dtype))

    def psum(self, banks):
        return self.enter_context(self.nc.psum_tensor(f"{self.tag}_ps", [P, banks, BANK], F32))

    def sem(self, name):
        sem = self.enter_context(self.nc.semaphore(f"{self.tag}_{name}"))
        assert sem.num not in Phase.last
        self.taken.add(sem.num)
        return sem

    def sems(self, names):
        return [self.sem(name) for name in names.split()]

    def block(self):
        return self.enter_context(self.nc.Block())


def wait_apart(eng, met, sem, value):
    value = eng.to_reg(value)
    eng.wait_ge(met, 1)
    eng.wait_ge(sem, value)


def halves(n):
    return [(a, min(BANK, n - a)) for a in range(0, n, BANK)]


def load_constants(nc, k):
    with Phase(nc, "const") as ph:
        par_loaded, pool_done, ident_ready = ph.sems("par_loaded pool_done ident_ready")
        block = ph.block()

        @block.sync
        def _(sp):
            sp.dma_start(k.par[:], k.d_par).then_inc(par_loaded, 16)
            sp.dma_start(k.x[:], k.d_x).then_inc(par_loaded, 16)
            sp.dma_start(k.ctx[:], k.d_ctx).then_inc(par_loaded, 16)
            sp.wait_ge(par_loaded, 48)

        @block.gpsimd
        def _(pool):
            pool.memset(k.ones[:], 1.0).then_inc(pool_done, 1)
            pool.memset(k.ident[:], 0.0).then_inc(pool_done, 1)
            pool.wait_ge(pool_done, 2)
            pool.affine_select(out=k.ident[:], in_=k.ident[:], compare_op=ALU.not_equal, fill=1.0, base=0,
                               pattern=[[-1, P]], channel_multiplier=1).then_inc(ident_ready, 1)

        @block.scalar
        def _(act):
            act.wait_ge(ident_ready, 1)
            act.copy(k.identr[:], k.ident[:])


def modulation(nc, k):
    GROUP = 4
    ROUNDS = NMOD * KT // GROUP // 2
    with Phase(nc, "ada") as ph:
        w = ph.sb("ada_w", [P, 2, GROUP, KT, P])
        sc = ph.sb("silu_c", [P, 2, KT])
        ps = ph.psum(2)
        loaded = [ph.sem(f"ada_loaded{s}") for s in range(2)]
        silu_ready, tiles_done = ph.sem("silu_ready"), ph.sem("ada_tiles_done")
        evicted, mod_ready = ph.sem("ada_evicted"), ph.sem("mod_ready")
        block = ph.block()

        @block.sync
        def _(sp):
            with sp.Fori(0, ROUNDS) as i:
                for s in range(2):
                    sp.wait_ge(tiles_done, 2 * i)
                    sp.dma_start(w[:, s], k.d_w_ada[2 * i + s]).then_inc(loaded[s], 16)

        @block.scalar
        def _(act):
            c0 = PAR["c"][0]
            act.activation(sc[:].rearrange("p v t -> p (v t)"), k.par[:, c0:c0 + 2 * KT], ACT.Silu).then_inc(silu_ready, 1)

        @block.tensor
        def _(pe):
            pe.wait_ge(silu_ready, 1)
            with pe.Fori(0, ROUNDS) as i:
                for s in range(2):
                    pe.wait_ge(evicted, 2 * i)
                    pe.wait_ge(loaded[s], 16 * (i + 1))
                    for t in range(GROUP):
                        for kt in range(KT):
                            mm = pe.matmul(ps[:, s, 2 * t:2 * t + 2], w[:, s, t, kt, :], sc[:, :, kt],
                                           start=kt == 0, stop=kt == KT - 1)
                    mm.then_inc(tiles_done, 1)

        @block.vector
        def _(dve):
            b0 = PAR["b_ada"][0]
            with dve.Fori(0, ROUNDS) as i:
                for s in range(2):
                    first = (2 * i + s) * GROUP
                    dve.wait_ge(tiles_done, 2 * i + s + 1)
                    dve.tensor_tensor(k.mod[:, bass.ds(first, GROUP), :],
                                      ps[:, s, 0:2 * GROUP].rearrange("p (t v) -> p t v", v=2),
                                      k.par[:, bass.ds(first + b0, GROUP)].unsqueeze(2).to_broadcast([P, GROUP, 2]),
                                      ALU.add).then_inc(evicted, 1)
            dve.wait_ge(evicted, 2 * ROUNDS)
            for n, (gain, scale, gate, half) in enumerate((("norm_ffn1", 1, 2, 0.5), ("norm_mix", 4, 5, 1.0),
                                                           ("norm_ffn2", 7, 8, 0.5))):
                g0 = PAR[gain][0]
                for v in range(2):
                    dve.scalar_tensor_tensor(out=k.gain[:, n, v, :], in0=k.mod[:, scale * KT:(scale + 1) * KT, v],
                                             scalar=1.0, in1=k.par[:, g0:g0 + KT], op0=ALU.add,
                                             op1=ALU.mult).then_inc(mod_ready, 1)
                    dve.tensor_scalar(k.gate[:, n, v, :], k.mod[:, gate * KT:(gate + 1) * KT, v], half, None,
                                      ALU.mult).then_inc(mod_ready, 1)


def norm(nc, k, tag, x, n, which=None, v=0, hi=None, lo=None, d_out=None):
    blocks = halves(n)
    final = d_out is not None
    with Phase(nc, tag) as ph:
        sq = ph.sb("sq", [P, 2, BANK])
        ms = ph.sb("mean_square", [P, BANK])
        inv = ph.sb("inv_ms", [P, BANK])
        rstd = ph.sb("rstd", [P, 2, BANK])
        xn = ph.sb("x_normed", [P, 2, BANK])
        h = ph.sb("h_whole", [P, 2, BANK])
        ps = ph.psum(2)
        sq_ready, sq_used, ms_ready, inv_ready, rstd_ready, xn_ready, h_ready, lo_ready, stored = ph.sems(
            "sq_ready sq_used ms_ready inv_ready rstd_ready xn_ready h_ready lo_ready stored")
        block = ph.block()

        @block.sync
        def _(sp):
            if final:
                for b, (t0, tn) in enumerate(blocks):
                    for kt in range(KT):
                        sp.wait_ge(xn_ready, b * KT + kt + 1)
                        sp.dma_start(d_out[:, kt, t0:t0 + tn], x[:, kt, t0:t0 + tn]).then_inc(stored, 16)
                sp.wait_ge(stored, 16 * KT * len(blocks))

        @block.scalar
        def _(act):
            for b, (t0, tn) in enumerate(blocks):
                for kt in range(KT):
                    i = b * KT + kt
                    if i >= 2:
                        act.wait_ge(sq_used, i - 1)
                    act.activation(sq[:, i % 2, 0:tn], x[:, kt, t0:t0 + tn], ACT.Square).then_inc(sq_ready, 1)
            for b, (t0, tn) in enumerate(blocks):
                act.wait_ge(inv_ready, b + 1)
                act.activation(rstd[:, b, 0:tn], inv[:, 0:tn], ACT.Sqrt).then_inc(rstd_ready, 1)
            for b, (t0, tn) in enumerate(blocks if not final else ()):
                for kt in range(KT):
                    i = b * KT + kt
                    scale, shift = k.gain[:, which, v, kt:kt + 1], k.mod[:, which * 3 * KT + kt, v:v + 1]
                    act.wait_ge(xn_ready, i + 1)
                    if i >= 2:
                        act.wait_ge(lo_ready, i - 1)
                    act.activation(h[:, i % 2, 0:tn], xn[:, i % 2, 0:tn], ACT.Identity, bias=shift, scale=scale)
                    act.activation(hi[:, kt, t0:t0 + tn], xn[:, i % 2, 0:tn], ACT.Identity, bias=shift,
                                   scale=scale).then_inc(h_ready, 1)

        @block.tensor
        def _(pe):
            for b, (t0, tn) in enumerate(blocks):
                for kt in range(KT):
                    pe.wait_ge(sq_ready, b * KT + kt + 1)
                    mm = pe.matmul(ps[:, b, 0:tn], k.ones[:], sq[:, kt % 2, 0:tn], start=kt == 0, stop=kt == KT - 1)
                    mm.then_inc(sq_used, 1)
        def split_lo(dve, i):
            b, kt = divmod(i, KT)
            t0, tn = blocks[b]
            dve.wait_ge(h_ready, i + 1)
            dve.tensor_tensor(lo[:, kt, t0:t0 + tn], h[:, i % 2, 0:tn], hi[:, kt, t0:t0 + tn].bitcast(F32),
                              ALU.subtract).then_inc(lo_ready, 1)

        @block.vector
        def _(dve):
            for b, (t0, tn) in enumerate(blocks):
                dve.wait_ge(sq_used, (b + 1) * KT)
                if b:
                    dve.wait_ge(inv_ready, b)
                dve.tensor_scalar(ms[:, 0:tn], ps[:, b, 0:tn], 1.0 / D, EPS, ALU.mult, ALU.add).then_inc(ms_ready, 1)
                dve.wait_ge(ms_ready, b + 1)
                if b:
                    dve.wait_ge(rstd_ready, b)
                dve.reciprocal(inv[:, 0:tn], ms[:, 0:tn]).then_inc(inv_ready, 1)
            for b, (t0, tn) in enumerate(blocks):
                dve.wait_ge(rstd_ready, b + 1)
                for kt in range(KT):
                    i = b * KT + kt
                    if final:
                        xs, g = x[:, kt, t0:t0 + tn], PAR["norm_final"][0] + kt
                        dve.scalar_tensor_tensor(out=xs, in0=xs, scalar=k.par[:, g:g + 1], in1=rstd[:, b, 0:tn],
                                                 op0=ALU.mult, op1=ALU.mult).then_inc(xn_ready, 1)
                        continue
                    if i >= 2:
                        dve.wait_ge(h_ready, i - 1)
                    dve.tensor_tensor(xn[:, i % 2, 0:tn], x[:, kt, t0:t0 + tn], rstd[:, b, 0:tn],
                                      ALU.mult).then_inc(xn_ready, 1)
                    if i >= 1:
                        split_lo(dve, i - 1)
            if not final:
                split_lo(dve, len(blocks) * KT - 1)


def three(pe, out, whi, wlo, ahi, alo, start, stop):
    pe.matmul(out, whi, alo, start=start, stop=False)
    pe.matmul(out, wlo, ahi, start=False, stop=False)
    return pe.matmul(out, whi, ahi, start=False, stop=stop)


def swiglu(nc, k, tag, x, n, which, v, hi, lo, d_w):
    blocks = halves(n)
    nb = len(blocks)
    rounds = FT // 2
    PIECES, RAW = 6, 3
    units = 2 * nb
    ys = KT * nb
    with Phase(nc, tag) as ph:
        raw = ph.sb("w_raw", [P, RAW, KT, P])
        wh = ph.sb("w_hi", [P, PIECES, KT, P], F32R)
        wl = ph.sb("w_lo", [P, PIECES, KT, P], F32R)
        ah = ph.sb("a_hi", [P, 2, n], F32R)
        al = ph.sb("a_lo", [P, 2, n], F32R)
        sg = ph.sb("silu_g", [P, 2, BANK])
        aw = ph.sb("a_whole", [P, 2, BANK])
        ps = ph.psum(8)
        loaded = [ph.sem(f"w_loaded{s}") for s in range(RAW)]
        hi_done = [ph.sem(f"w_hi_done{s}") for s in range(RAW)]
        lo_done = [ph.sem(f"w_lo_done{s}") for s in range(RAW)]
        gu_ready = [ph.sem(s) for s in ("gate_ready", "up_ready")]
        y_ready, y_added = [ph.sem(s) for s in ("y_ready", "y_added")]
        sg_ready, aw_ready, ah_ready, al_ready = [
            ph.sem(s) for s in ("silu_ready", "a_ready", "a_hi_ready", "a_lo_ready")]
        block = ph.block()

        @block.sync
        def _(sp):
            with sp.Fori(0, rounds) as g:
                for j in range(PIECES):
                    sp.wait_ge(hi_done[j % RAW], 2 * g + j // RAW)
                    sp.wait_ge(lo_done[j % RAW], 2 * g + j // RAW)
                    sp.dma_start(raw[:, j % RAW], d_w[PIECES * g + j]).then_inc(loaded[j % RAW], 16)

        def split_hi(act, g, j, first=False):
            s = j % RAW
            if not first:
                act.wait_ge(*((gu_ready[j % 2], units * (g - 1) + (j // 2 + 1) * nb) if j < 4 else (y_ready, ys * g)))
            act.wait_ge(loaded[s], 16 * (2 * g + j // RAW + 1))
            act.copy(wh[:, j], raw[:, s]).then_inc(hi_done[s], 1)

        def split_lo(dve, g, j):
            s = j % RAW
            dve.wait_ge(hi_done[s], 2 * g + j // RAW + 1)
            dve.tensor_tensor(wl[:, j], raw[:, s], wh[:, j].bitcast(F32), ALU.subtract).then_inc(lo_done[s], 1)

        def ahead(u):
            return [] if u < nb else [0, 1] if nb == 1 else [u - nb]

        def act_round(act, g, last):
            for u in range(units):
                f, (t0, tn) = u // nb, blocks[u % nb]
                act.wait_ge(gu_ready[0], units * g + u + 1)
                act.activation(sg[:, u % 2, 0:tn], ps[:, 2 * (u % 2), 0:tn], ACT.Silu).then_inc(sg_ready, 1)
                if u % nb == 0:
                    split_hi(act, g, 4 + f)
                act.wait_ge(aw_ready, units * g + u + 1)
                act.copy(ah[:, f, t0:t0 + tn], aw[:, u % 2, 0:tn]).then_inc(ah_ready, 1)
                for j in () if last else ahead(u):
                    split_hi(act, g + 1, j)
            for j in () if last else (2, 3):
                split_hi(act, g + 1, j)

        @block.scalar
        def _(act):
            for j in range(4):
                split_hi(act, 0, j, first=True)
            with act.Fori(0, rounds - 1) as g:
                act_round(act, g, False)
            act_round(act, rounds - 1, True)

        def dve_round(dve, g, last):
            for u in range(units):
                f, (t0, tn) = u // nb, blocks[u % nb]
                dve.wait_ge(gu_ready[1], units * g + u + 1)
                dve.wait_ge(sg_ready, units * g + u + 1)
                dve.tensor_tensor(aw[:, u % 2, 0:tn], sg[:, u % 2, 0:tn], ps[:, 2 * (u % 2) + 1, 0:tn],
                                  ALU.mult).then_inc(aw_ready, 1)
                if u % nb == 0:
                    split_lo(dve, g, 4 + f)
                dve.wait_ge(ah_ready, units * g + u + 1)
                dve.tensor_tensor(al[:, f, t0:t0 + tn], aw[:, u % 2, 0:tn], ah[:, f, t0:t0 + tn].bitcast(F32),
                                  ALU.subtract).then_inc(al_ready, 1)
                for j in () if last else ahead(u):
                    split_lo(dve, g + 1, j)
            for y in range(ys):
                o, (t0, tn) = y % KT, blocks[y // KT]
                xs = x[:, o, t0:t0 + tn]
                dve.wait_ge(y_ready, ys * g + y + 1)
                dve.scalar_tensor_tensor(out=xs, in0=ps[:, 4 + y % 4, 0:tn], scalar=k.gate[:, which, v, o:o + 1],
                                         in1=xs, op0=ALU.mult, op1=ALU.add).then_inc(y_added, 1)
                if not last and y % (ys // 2) == 0:
                    split_lo(dve, g + 1, 2 + y // (ys // 2))

        @block.vector
        def _(dve):
            for j in range(4):
                split_lo(dve, 0, j)
            with dve.Fori(0, rounds - 1) as g:
                dve_round(dve, g, False)
            dve_round(dve, rounds - 1, True)

        @block.tensor
        def _(pe):
            with pe.Fori(0, rounds) as g:
                for u in range(units):
                    f, (t0, tn) = u // nb, blocks[u % nb]
                    for half in range(2):
                        j = 2 * f + half
                        if u % nb == 0:
                            pe.wait_ge(lo_done[j % RAW], 2 * g + j // RAW + 1)
                        pe.wait_ge(aw_ready, units * g + max(u - 1, 0))
                        for kt in range(KT):
                            mm = three(pe, ps[:, 2 * (u % 2) + half, 0:tn], wh[:, j, kt], wl[:, j, kt],
                                       hi[:, kt, t0:t0 + tn], lo[:, kt, t0:t0 + tn], kt == 0, kt == KT - 1)
                        mm.then_inc(gu_ready[half], 1)
                for f in range(2):
                    pe.wait_ge(lo_done[(4 + f) % RAW], 2 * g + (4 + f) // RAW + 1)
                for y in range(ys):
                    (b, o), (t0, tn) = divmod(y, KT), blocks[y // KT]
                    if o == 0:
                        pe.wait_ge(al_ready, units * g + nb + b + 1)
                    pe.wait_ge(y_added, ys * g + max(y - 3, 0))
                    for f in range(2):
                        mm = three(pe, ps[:, 4 + y % 4, 0:tn], wh[:, 4 + f, o], wl[:, 4 + f, o],
                                   ah[:, f, t0:t0 + tn], al[:, f, t0:t0 + tn], f == 0, f == 1)
                    mm.then_inc(y_ready, 1)


def project(nc, k, tag, n_tiles, d_w, srcs, kind, d_out=None, par0=None):
    nb = len(srcs)
    n = sum(s[2] for s in srcs)
    at = [sum(s[2] for s in srcs[:b]) for b in range(nb)]
    shift, residual = kind == "shift", kind == "residual"
    rounds = (n_tiles - 1) // 2
    tail = range(2 * rounds, n_tiles)
    with Phase(nc, tag) as ph:
        raw = ph.sb("w_raw", [P, 2, KT, P])
        wh, wl = ph.sb("w_hi", [P, 2, KT, P], F32R), ph.sb("w_lo", [P, 2, KT, P], F32R)
        if not residual:
            stage = ph.sb("stage", [P, 2, n])
        if shift:
            pad = ph.sb("padded", [P, TOK + 3])
            rest = ph.sb("mu_rest", [P, RW_TILES])
            segments = ((1, 0, CTX), (CTX + 2, CTX, SEQ))
            pad_at = (CTX + 2, CTX + 2 + BANK, 1)
        ps = ph.psum(2 * nb)
        loaded = [ph.sem(f"w_loaded{s}") for s in range(2)]
        stored = [ph.sem(f"stored{s}") for s in range(2)]
        hi_done, lo_done, out_ready, evicted, added, shift_step, pads_ready = ph.sems(
            "w_hi_done w_lo_done out_ready evicted added shift_step pads_ready")
        block = ph.block()

        def load(sp, t, s, first=False):
            if not first:
                sp.wait_ge(lo_done, t - 1)
            sp.dma_start(raw[:, s], d_w[t]).then_inc(loaded[s], 16)

        def store(sp, t, s):
            if residual:
                return
            if shift:
                sp.wait_ge(shift_step, 6 * (t + 1) + 1)
                sp.dma_start(d_out[t][:, TOK:], stage[:, s, 0:CTX]).then_inc(stored[s], 16)
            else:
                sp.wait_ge(evicted, nb * (t + 1))
            sp.dma_start(d_out[t][:, 0:n], stage[:, s, :]).then_inc(stored[s], 16)

        def stores_before(i):
            return i * (32 if shift else 16)

        @block.sync
        def _(sp):
            load(sp, 0, 0, first=True)
            with sp.Fori(0, rounds) as i:
                load(sp, 2 * i + 1, 1)
                load(sp, 2 * i + 2, 0)
                store(sp, 2 * i, 0)
                store(sp, 2 * i + 1, 1)
            if n_tiles % 2 == 0:
                load(sp, n_tiles - 1, 1)
            for t in tail:
                store(sp, t, t % 2)
            if not residual:
                for s in range(2):
                    sp.wait_ge(stored[s], stores_before(len(range(s, n_tiles, 2))))

        def split_hi(act, t, s, i, first=False):
            if not first:
                act.wait_ge(out_ready, nb * (t - 1))
            act.wait_ge(loaded[s], 16 * (i + 1))
            act.copy(wh[:, s], raw[:, s]).then_inc(hi_done, 1)

        def evict(act, t, s, i):
            if residual:
                return
            if shift:
                act.wait_ge(shift_step, 6 * t + 1)
            else:
                act.wait_ge(stored[s], stores_before(i))
            for b, (_, _, tn) in enumerate(srcs):
                src = ps[:, s * nb + b, 0:tn]
                wait_apart(act, hi_done, out_ready, nb * t + b + 1)
                if shift:
                    act.copy(pad[:, pad_at[b]:pad_at[b] + tn], src).then_inc(evicted, 1)
                elif kind == "gate":
                    act.activation(stage[:, s, at[b]:at[b] + tn], src, ACT.Sigmoid,
                                   bias=k.par[:, bass.ds(t + par0, 1)]).then_inc(evicted, 1)
                else:
                    act.mul(stage[:, s, at[b]:at[b] + tn], src, par0).then_inc(evicted, 1)

        @block.scalar
        def _(act):
            split_hi(act, 0, 0, 0, first=True)
            if shift:
                act.wait_ge(pads_ready, 3)
            with act.Fori(0, rounds) as i:
                split_hi(act, 2 * i + 1, 1, i)
                evict(act, 2 * i, 0, i)
                split_hi(act, 2 * i + 2, 0, i + 1)
                evict(act, 2 * i + 1, 1, i)
            for t in tail:
                if t + 1 < n_tiles:
                    split_hi(act, t + 1, (t + 1) % 2, (t + 1) // 2)
                evict(act, t, t % 2, t // 2)

        def split_lo(dve, t, s):
            dve.wait_ge(hi_done, t + 1)
            dve.tensor_tensor(wl[:, s], raw[:, s], wh[:, s].bitcast(F32), ALU.subtract).then_inc(lo_done, 1)

        def finish(dve, t, s, i):
            if residual:
                for b, (_, _, tn) in enumerate(srcs):
                    xs = k.x[:, bass.ds(t, 1), at[b]:at[b] + tn].squeeze(1)
                    dve.wait_ge(out_ready, nb * t + b + 1)
                    dve.scalar_tensor_tensor(out=xs, in0=ps[:, s * nb + b, 0:tn], scalar=k.gate[:, 1, 0, bass.ds(t, 1)],
                                             in1=xs, op0=ALU.mult, op1=ALU.add).then_inc(added, 1)
            if shift:
                mp, mn = PAR["mu_prev"][0], PAR["mu_next"][0]
                dve.wait_ge(evicted, nb * (t + 1))
                dve.wait_ge(stored[s], stores_before(i))
                for a, o, m in segments:
                    dve.tensor_scalar(stage[:, s, o:o + m], pad[:, a:a + m], rest[:, bass.ds(t, 1)], None,
                                      ALU.mult).then_inc(shift_step, 1)
                for step, (mu, d) in enumerate(((mp, -1), (mn, 1))):
                    for q, (a, o, m) in enumerate(segments):
                        dve.wait_ge(shift_step, 6 * t + 2 * step + q + 2)
                        dve.scalar_tensor_tensor(out=stage[:, s, o:o + m], in0=pad[:, a + d:a + d + m],
                                                 scalar=k.par[:, bass.ds(t + mu, 1)], in1=stage[:, s, o:o + m],
                                                 op0=ALU.mult, op1=ALU.add).then_inc(shift_step, 1)

        @block.vector
        def _(dve):
            if shift:
                mp, mn = PAR["mu_prev"][0], PAR["mu_next"][0]
                for z in (0, CTX + 1, TOK + 2):
                    dve.memset(pad[:, z:z + 1], 0.0).then_inc(pads_ready, 1)
                dve.tensor_tensor(rest[:], k.par[:, mp:mp + RW_TILES], k.par[:, mn:mn + RW_TILES],
                                  ALU.add).then_inc(pads_ready, 1)
                dve.wait_ge(pads_ready, 4)
                dve.tensor_scalar(rest[:], rest[:], -1.0, 1.0, ALU.mult, ALU.add).then_inc(shift_step, 1)
                dve.wait_ge(shift_step, 1)
            split_lo(dve, 0, 0)
            with dve.Fori(0, rounds) as i:
                split_lo(dve, 2 * i + 1, 1)
                finish(dve, 2 * i, 0, i)
                split_lo(dve, 2 * i + 2, 0)
                finish(dve, 2 * i + 1, 1, i)
            for t in tail:
                if t + 1 < n_tiles:
                    split_lo(dve, t + 1, (t + 1) % 2)
                finish(dve, t, t % 2, t // 2)

        def product(pe, t, s, i):
            pe.wait_ge(lo_done, t + 1)
            pe.wait_ge(added if residual else evicted, nb * 2 * i)
            if s:
                pe.wait_ge(added if residual else evicted, nb * (2 * i + s - 1))
            for b, (h_hi, h_lo, tn) in enumerate(srcs):
                for kt in range(KT):
                    mm = three(pe, ps[:, s * nb + b, 0:tn], wh[:, s, kt], wl[:, s, kt], h_hi[:, kt], h_lo[:, kt],
                               kt == 0, kt == KT - 1)
                mm.then_inc(out_ready, 1)

        @block.tensor
        def _(pe):
            with pe.Fori(0, rounds) as i:
                for s in range(2):
                    product(pe, 2 * i + s, s, i)
            for t in tail:
                product(pe, t, t % 2, t // 2)


def project_v(nc, k, hi, lo, hi_c, lo_c, d_w, d_out):
    n_tiles = TOK // P
    NV = HEADS * HD
    with Phase(nc, "pv") as ph:
        raw = ph.sb("w_raw", [P, KT, NV])
        wh, wl = ph.sb("w_hi", [P, KT, NV], F32R), ph.sb("w_lo", [P, KT, NV], F32R)
        stage = ph.sb("stage", [P, 2, NV])
        ps = ph.psum(4)
        loaded, hi_done, lo_done, out_ready, evicted = ph.sems("w_loaded w_hi_done w_lo_done out_ready evicted")
        stored = [ph.sem(f"stored{s}") for s in range(2)]
        block = ph.block()
        QUARTERS = [range(q, q + 2) for q in range(0, KT, 2)]

        @block.sync
        def _(sp):
            for q in QUARTERS:
                sp.dma_start(raw[:, q[0]:q[-1] + 1], d_w[:, q[0]:q[-1] + 1]).then_inc(loaded, 16)
                sp.wait_ge(loaded, 16 * (q[0] // 2 + 1))
            for t in range(n_tiles):
                sp.wait_ge(evicted, t + 1)
                sp.dma_start(d_out[t], stage[:, t % 2]).then_inc(stored[t % 2], 16)
            for s in range(2):
                sp.wait_ge(stored[s], 16 * (n_tiles // 2))

        @block.scalar
        def _(act):
            for i, q in enumerate(QUARTERS):
                act.wait_ge(loaded, 16 * (i + 1))
                act.copy(wh[:, q[0]:q[-1] + 1], raw[:, q[0]:q[-1] + 1]).then_inc(hi_done, 1)
            for t in range(n_tiles):
                act.wait_ge(out_ready, t + 1)
                if t >= 2:
                    act.wait_ge(stored[t % 2], 16 * (t // 2))
                act.copy(stage[:, t % 2], ps[:, t % 4]).then_inc(evicted, 1)

        @block.vector
        def _(dve):
            for i, q in enumerate(QUARTERS):
                a, b = q[0], q[-1] + 1
                dve.wait_ge(hi_done, i + 1)
                dve.tensor_tensor(wl[:, a:b], raw[:, a:b], wh[:, a:b].bitcast(F32), ALU.subtract).then_inc(lo_done, 1)

        @block.tensor
        def _(pe):
            for t in range(n_tiles):
                h, l, a = (hi, lo, t * P) if t < SEQ // P else (hi_c, lo_c, t * P - SEQ)
                if t >= 4:
                    pe.wait_ge(evicted, t - 3)
                for kt in range(KT):
                    if t == 0 and kt % 2 == 0:
                        pe.wait_ge(lo_done, kt // 2 + 1)
                    mm = three(pe, ps[:, t % 4], h[:, kt, a:a + P], l[:, kt, a:a + P], wh[:, kt], wl[:, kt],
                               kt == 0, kt == KT - 1)
                mm.then_inc(out_ready, 1)


def attention(nc, k, d_q, d_k, d_v, d_rpb):
    PAIRS = ROWS // 2
    E = 2 * WIN_H
    LOC = (WIN_H + 1) * GRID_W
    TILES = TOK // P

    def window(p):
        i = 2 * p
        r0, r1 = (min(max(r - WIN_H // 2, 0), ROWS - WIN_H) for r in (i, i + 1))
        return r0, r1 - r0 + WIN_H, r0 - i + WIN_H - 1

    with Phase(nc, "na") as ph:
        q, kk, vv = ph.sb("q", [P, HP, SEQ]), ph.sb("k", [P, HP, TOK]), ph.sb("v", [P, TILES, HEADS * HD])
        qz = ph.sb("q_of_head", [P, 2, SEQ])
        rpb = ph.sb("rpb", [P, HP, 2, E, GRID_W])
        edge = ph.sb("bias_edge", [P, 2, E, GRID_W])
        inner = ph.sb("bias_inner", [P, 2, WIN_H + 1, GRID_W])
        outside = ph.sb("outside", [P, WIN_H + 1, GRID_W])
        sb_ = ph.sb("s_biased", [P, 2, LOC])
        pr = ph.sb("probs", [P, 2, LOC + CTX])
        prT = ph.sb("probs_t", [P, 2, 7, P])
        o = ph.sb("o", [P, 2, P])
        stat = ph.sb("stat", [P, 2, 8])
        ps = ph.psum(8)
        S_BANK, T_BANK, O_BANK, OT_BANK = (0, 2), 4, 6, 7
        (in_loaded, rpb_loaded, bias_built, mask_step, qz_ready, s_ready, m_step, neg_ready, e_ready,
         t_ready, pt_dve, pt_act, o_ready, o_scaled, den_step, ot_ready, ot_done, zeroed, mask_copied) = ph.sems(
            "in_loaded rpb_loaded bias_built mask_step qz_ready s_ready m_step neg_ready e_ready t_ready "
            "pt_dve pt_act o_ready o_scaled den_step ot_ready ot_done zeroed mask_copied")
        block = ph.block()
        U = 2 * PAIRS
        units = [(p, s) for p in range(PAIRS) for s in range(2)]

        @block.sync
        def _(sp):
            for hp in range(HP):
                sp.dma_start(q[:, hp], d_q[hp]).then_inc(in_loaded, 16)
                sp.dma_start(kk[:, hp], d_k[hp]).then_inc(in_loaded, 16)
            sp.dma_start(vv[:], d_v.rearrange("t p c -> p t c")).then_inc(in_loaded, 16)
            for h in range(HEADS):
                for row in range(2):
                    sp.dma_start(rpb[row * GRID_W:(row + 1) * GRID_W, h // 2, h % 2],
                                 d_rpb[h][:, 1 - row:1 - row + E]).then_inc(rpb_loaded, 16)
            sp.wait_ge(rpb_loaded, 32 * HEADS)

        @block.gpsimd
        def _(pool):
            first, lim, back = outside[0:GRID_W], GRID_W - WIN_W, WIN_W // 2
            pool.memset(outside[:], 0.0).then_inc(mask_step, 1)
            pool.wait_ge(mask_step, 1)
            pool.affine_select(out=first[:, :, 0:lim], in_=first[:, :, 0:lim], compare_op=ALU.is_ge, fill=MASKED,
                               base=back, pattern=[[0, WIN_H + 1], [1, lim]],
                               channel_multiplier=-1).then_inc(mask_step, 1)
            pool.wait_ge(mask_step, 2)
            pool.affine_select(out=first[:, :, WIN_W:], in_=first[:, :, WIN_W:], compare_op=ALU.is_ge, fill=MASKED,
                               base=-back - 1, pattern=[[0, WIN_H + 1], [-1, lim]],
                               channel_multiplier=1).then_inc(mask_step, 1)
            pool.wait_ge(mask_step, 3)
            pool.dma_start(outside[GRID_W:P], first).then_inc(mask_copied, 16)
            pool.wait_ge(mask_copied, 16)
            pool.memset(outside[0:GRID_W, WIN_H], MASKED).then_inc(mask_step, 1)
            pool.memset(outside[GRID_W:P, 0], MASKED).then_inc(mask_step, 1)

        MASK_STEPS = 5

        @block.scalar
        def _(act):
            act.wait_ge(in_loaded, 16 * (2 * HP + 1))
            act.wait_ge(zeroed, 2)
            with act.Fori(0, HP) as hp:
                for s in range(2):
                    a, b = s * HD, (s + 1) * HD
                    act.wait_ge(s_ready, U * hp)
                    act.copy(qz[a:b, s, :], q[a:b, bass.ds(hp, 1), :].squeeze(1)).then_inc(qz_ready, 1)

                def exps(u):
                    p, s = units[u]
                    L = window(p)[1] * GRID_W
                    act.wait_ge(neg_ready, U * hp + u + 1)
                    if u >= 2:
                        act.wait_ge(t_ready, U * hp + u - 1)
                    else:
                        act.wait_ge(t_ready, U * hp)
                    act.activation(pr[:, s, 0:L], sb_[:, s, 0:L], ACT.Exp, bias=stat[:, s, 2:3],
                                   accum_out=stat[:, s, 3:4])
                    act.activation(pr[:, s, L:L + CTX], ps[:, S_BANK[s] + 1, BANK - CTX:BANK], ACT.Exp,
                                   bias=stat[:, s, 2:3], accum_out=stat[:, s, 4:5]).then_inc(e_ready, 1)

                def probs_t(u):
                    act.wait_ge(t_ready, U * hp + u + 1)
                    act.copy(prT[:, units[u][1], 4:7], ps[:, T_BANK + 1, 0:3 * P].rearrange("p (t q) -> p t q", q=P)).then_inc(pt_act, 1)

                for u in range(U + 1):
                    if u < U:
                        exps(u)
                    if u >= 1:
                        probs_t(u - 1)

        @block.vector
        def _(dve):
            for s in range(2):
                dve.memset(qz[(1 - s) * HD:(2 - s) * HD, s, :], 0.0).then_inc(zeroed, 1)
            dve.memset(ps[:, T_BANK + 1, 0:3 * P], 0.0).then_inc(zeroed, 1)
            dve.wait_ge(mask_step, MASK_STEPS)
            dve.wait_ge(rpb_loaded, 32 * HEADS)
            with dve.Fori(0, HP) as hp:
                raw_bias = rpb[:, bass.ds(hp, 1)].squeeze(1)
                for s in range(2):
                    dve.tensor_tensor(edge[:, s], raw_bias[:, s], outside[:, 1:2, :].to_broadcast([P, E, GRID_W]),
                                      ALU.add).then_inc(bias_built, 1)
                    dve.tensor_tensor(inner[:, s], raw_bias[:, s, WIN_H // 2 - 1:WIN_H // 2 + WIN_H], outside[:],
                                      ALU.add).then_inc(bias_built, 1)
                dve.wait_ge(bias_built, 4 * (hp + 1))

                def biased(u):
                    p, s = units[u]
                    r0, rows, e0 = window(p)
                    L = rows * GRID_W
                    table = edge[:, s, e0:e0 + rows] if rows == WIN_H else inner[:, s]
                    dve.wait_ge(s_ready, U * hp + u + 1)
                    S = ps[:, S_BANK[s]:S_BANK[s] + 2].rearrange("p b c -> p (b c)")
                    dve.tensor_reduce(stat[:, s, 0:1], S[:, 2 * BANK - CTX:], AX.X, ALU.max).then_inc(m_step, 1)
                    wait_apart(dve, bias_built, e_ready, U * hp + max(u - 1, 0))
                    dve.tensor_tensor_reduce(out=sb_[:, s, 0:L], in0=S[:, 0:L], in1=table.rearrange("p r c -> p (r c)"),
                                             scale=1.0, scalar=MASKED, op0=ALU.add, op1=ALU.max,
                                             accum_out=stat[:, s, 1:2]).then_inc(m_step, 1)
                    dve.wait_ge(m_step, 2 * (U * hp + u + 1))
                    dve.tensor_scalar(stat[:, s, 2:3], stat[:, s, 1:2], stat[:, s, 0:1], -1.0, ALU.max,
                                      ALU.mult).then_inc(neg_ready, 1)

                def probs_t(u):
                    dve.wait_ge(t_ready, U * hp + u + 1)
                    dve.tensor_copy(prT[:, units[u][1], 0:4], ps[:, T_BANK].rearrange("p (t q) -> p t q", q=P)).then_inc(pt_dve, 1)
                    s = units[u][1]
                    dve.wait_ge(e_ready, U * hp + u + 1)
                    dve.tensor_tensor(stat[:, s, 5:6], stat[:, s, 3:4], stat[:, s, 4:5], ALU.add).then_inc(den_step, 1)
                    dve.wait_ge(den_step, 2 * (U * hp + u) + 1)
                    dve.reciprocal(stat[:, s, 6:7], stat[:, s, 5:6]).then_inc(den_step, 1)

                def scaled(u):
                    p, s = units[u]
                    dve.wait_ge(o_ready, U * hp + u + 1)
                    dve.wait_ge(den_step, 2 * (U * hp + u + 1))
                    if p >= 2:
                        dve.wait_ge(ot_ready, PAIRS * hp + p - 1)
                    else:
                        dve.wait_ge(ot_ready, PAIRS * hp)
                    dve.tensor_scalar(o[:, p % 2, s * HD:(s + 1) * HD], ps[:, O_BANK, 0:HD], stat[:, s, 6:7], None,
                                      ALU.mult).then_inc(o_scaled, 1)

                def out(p):
                    dve.wait_ge(ot_ready, PAIRS * hp + p + 1)
                    dve.tensor_copy(k.o_na[:, bass.ds(hp, 1), p * P:(p + 1) * P].squeeze(1),
                                    ps[:, OT_BANK, 0:P]).then_inc(ot_done, 1)

                for u in range(U + 3):
                    if u < U:
                        biased(u)
                    if 1 <= u <= U:
                        probs_t(u - 1)
                    if 2 <= u < U + 2:
                        scaled(u - 2)
                    if u >= 4 and u % 2 == 0:
                        out((u - 4) // 2)

        @block.tensor
        def _(pe):
            pe.wait_ge(in_loaded, 16 * (2 * HP + 1))
            pe.wait_ge(zeroed, 3)
            with pe.Fori(0, HP) as hp:
                def scores(u):
                    p, s = units[u]
                    r0, rows, _ = window(p)
                    if u < 2:
                        pe.wait_ge(qz_ready, 2 * hp + s + 1)
                        pe.wait_ge(e_ready, U * hp)
                    else:
                        pe.wait_ge(e_ready, U * hp + u - 1)
                    lhs = qz[:, s, p * P:(p + 1) * P]
                    keys = kk[:, bass.ds(hp, 1), :].squeeze(1)
                    a = r0 * GRID_W
                    pe.matmul(ps[:, S_BANK[s]], lhs, keys[:, a:a + BANK], start=True, stop=True)
                    if rows > WIN_H:
                        pe.matmul(ps[:, S_BANK[s] + 1, 0:GRID_W], lhs, keys[:, a + BANK:a + BANK + GRID_W],
                                  start=True, stop=True)
                    pe.matmul(ps[:, S_BANK[s] + 1, BANK - CTX:BANK], lhs, keys[:, SEQ:TOK], start=True,
                              stop=True).then_inc(s_ready, 1)

                def blocks(u):
                    r0, rows, _ = window(units[u][0])
                    L = rows * GRID_W
                    loc = [(c, min(P, L - c), r0 // 2 + c // P) for c in range(0, L, P)]
                    return loc + [(L + c, P, (SEQ + c) // P) for c in range(0, CTX, P)]

                def transposes(u):
                    s = units[u][1]
                    pe.wait_ge(e_ready, U * hp + u + 1)
                    pe.wait_ge(pt_dve, U * hp + u)
                    pe.wait_ge(pt_act, U * hp + u)
                    for j, (c, m, _) in enumerate(blocks(u)):
                        mm = pe.transpose(ps[0:m, T_BANK + j // 4, (j % 4) * P:(j % 4 + 1) * P], pr[:, s, c:c + m],
                                          k.ident[:])
                    mm.then_inc(t_ready, 1)

                def values(u):
                    s = units[u][1]
                    pe.wait_ge(pt_dve, U * hp + u + 1)
                    pe.wait_ge(pt_act, U * hp + u + 1)
                    pe.wait_ge(o_scaled, U * hp + u)
                    bl = blocks(u)
                    for j, (_, m, t) in enumerate(bl):
                        mm = pe.matmul(ps[:, O_BANK, 0:HD], prT[0:m, s, j], vv[0:m, t, bass.ds(hp * P + s * HD, HD)],
                                       start=j == 0, stop=j == len(bl) - 1)
                    mm.then_inc(o_ready, 1)

                def out(p):
                    pe.wait_ge(o_scaled, U * hp + 2 * p + 2)
                    pe.wait_ge(ot_done, PAIRS * hp + p)
                    pe.transpose(ps[:, OT_BANK, 0:P], o[:, p % 2], k.ident[:]).then_inc(ot_ready, 1)

                for u in range(U + 3):
                    if u < U:
                        scores(u)
                    if 1 <= u <= U:
                        transposes(u - 1)
                    if 2 <= u < U + 2:
                        values(u - 2)
                    if u >= 4 and u % 2 == 0:
                        out((u - 4) // 2)


LEVELS = 7


def rwkv_masks(nc, k):
    with Phase(nc, "masks") as ph:
        work = ph.sb("work", [P, 2 * LEVELS + 6, P])
        same = ph.sb("same", [P, LEVELS + 1, P])
        step, tables_copied = ph.sems("pool_step tables_copied")
        block = ph.block()

        @block.sync
        def _(sp):
            sp.dma_start(k.d_rpb_copies, k.d_rpb_source).then_inc(tables_copied, 16)
            sp.wait_ge(tables_copied, 16)

        @block.gpsimd
        def _(pool):
            steps = Chain(pool, step)

            def select(out, in_, op, base, pattern, mult):
                steps.done(pool.affine_select(out=out, in_=in_, compare_op=op, fill=0.0, base=base, pattern=pattern,
                                              channel_multiplier=mult))

            def blocks_of(out, size):
                v = out.rearrange("p (b c) -> p b c", c=size)
                steps.done(pool.memset(out, 1.0))
                steps.wait()
                select(v, v, ALU.is_ge, 0, [[-size, P // size], [0, size]], 1)
                steps.wait()
                select(v, v, ALU.is_ge, size - 1, [[size, P // size], [0, size]], -1)
                steps.wait()

            for l in range(LEVELS + 1):
                blocks_of(same[:, l], 1 << l)
            steps.done(pool.tensor_copy(k.same64[:], same[:, 6]))
            lower, upper = (1, [[-1, P]]), (-1, [[1, P]])
            w = 0
            for d in range(2):
                mult, pattern = (upper, lower)[d]
                for inclusive in range(2):
                    t = work[:, w]
                    w += 1
                    select(t, same[:, LEVELS], ALU.is_ge, inclusive - 1, pattern, mult)
                    steps.wait()
                    for h in range(2):
                        steps.done(pool.tensor_copy(k.keep[:, d, h, inclusive], t))
                mult, pattern = (lower, upper)[d]
                for l in range(LEVELS):
                    t = work[:, w % (2 * LEVELS + 6)]
                    w += 1
                    steps.done(pool.tensor_tensor(t, same[:, l + 1], same[:, l], ALU.subtract))
                    steps.wait()
                    select(t, t, ALU.is_ge, 0, pattern, mult)
                    steps.wait()
                    steps.done(pool.tensor_tensor(k.level[:, d, l], t, k.ident[:], ALU.add))


def rwkv(nc, k, d_rw, d_wup, d_aup, d_gup):
    L = NCH * CH
    OFF = (0, CTX)
    MID = (CH // 2 - 1, CH // 2)
    END = (CH - 1, 0)
    SC = STREAM // CH
    TS = 2 * LEVELS - 1
    BLOCKS, SBLOCKS = halves(L), halves(STREAM)
    NZ = 4 * len(BLOCKS)
    DVE_PER_PAIR = 42
    with Phase(nc, "rw") as ph:
        tw, al = ph.sb("tanh_w", [P, STREAM]), ph.sb("a_in", [P, STREAM])
        sgl = ph.sb("sigmoid_g", [P, SEQ])
        r, kf, v = ph.sb("r", [P, STREAM]), ph.sb("k", [P, STREAM]), ph.sb("v", [P, STREAM])
        kk = ph.sb("kk", [P, STREAM])
        ytok = kk[:].rearrange("p (c f) -> p c f", f=CH)
        vtok = ph.sb("v_tok", [P, SC, CH])
        ar = ph.sb("alpha_rho", [P, 2, 2, L])
        bk = ph.sb("beta_kappa", [P, 2, 2, L])
        e = ph.sb("e", [P, L])
        small = ph.sb("decays", [P, 2, 4, NCH])
        lw, la = ph.sb("w_up", [P, 2, P]), ph.sb("a_up", [P, 2, P])
        gup = ph.sb("g_up", [P, P])
        rest = ph.sb("rest", [P, HP])
        stat = ph.sb("gn_stat", [P, 4, 2 * SEQ // P])
        ar_s, arz = ph.sb("ar_s", [P, 2, 2, CH]), ph.sb("ar_of_head", [P, 2, 2, 2, CH])
        bk_s, bke = ph.sb("bk_s", [P, 2, 2, CH]), ph.sb("bk_end", [P, 2, 2, CH])
        bket = ph.sb("bk_end_tok", [P, 2, 2, CH])
        ab, kr = ph.sb("ab", [P, 2, 2, 2, CH]), ph.sb("kr", [P, 2, 2, 2, CH])
        atr = ph.sb("a_t", [P, 2, 2, CH], F32R)
        tb, ttb = ph.sb("t_inv", [P, 2, 2, CH], F32R), ph.sb("t_inv_t", [P, 2, 2, CH], F32R)
        pl = ph.sb("joined", [P, 2, 2, 2, CH], F32R)
        it = ph.sb("i_minus_t", [P, 2, 2, CH])
        er = ph.sb("residual", [P, 2, 2, CH], F32R)
        ttf = ph.sb("t_newton_t", [P, 2, 2, CH])
        wsb, usb, sbd = ph.sb("w", [P, 2, CH]), ph.sb("u", [P, 2, CH]), ph.sb("state", [P, 2, P])
        ps = ph.psum(8)

        def bank(d, i):
            return ps[:, 4 * d + i]

        def flat(a):
            return a.rearrange("p h t -> p (h t)")

        (lora_loaded, hp_loaded, lora_ready, zeroed, go, sq_ready, kk_sum, kk_inv, kk_rstd, za_ready, za_evicted,
         bonus_in, bonus_ps, log_ready, e_ready, ar_ready, vt_ready, vt_copied, bulk_ready, centred, gn_sq, gn_inv,
         gn_rstd, normed, ln_ps, ln_done, gate_ps, pair_done, dve_step) = ph.sems(
            "lora_loaded hp_loaded lora_ready zeroed go sq_ready kk_sum kk_inv kk_rstd za_ready za_evicted "
            "bonus_in bonus_ps log_ready e_ready ar_ready vt_ready vt_copied bulk_ready centred gn_sq gn_inv "
            "gn_rstd normed ln_ps ln_done gate_ps pair_done dve_step")

        def per_dir(names):
            return [[ph.sem(f"{name}{d}") for d in range(2)] for name in names.split()]

        (staged, arz_ready, m_ready, masked, at_ready, bke_ready, tr_ready, tr_copied, p_ready, pl_ready, t_ready,
         t_copied, g_ready, er_ready, n_ready, ttf_ready, w_ready, w_copied, u_ready, u_copied, st_ready,
         st_done, y_ready, y_added, it_ready) = per_dir(
            "staged arz_ready m_ready masked at_ready bke_ready tr_ready tr_copied p_ready pl_ready t_ready t_copied "
            "g_ready er_ready n_ready ttf_ready w_ready w_copied u_ready u_copied st_ready st_done y_ready y_added "
            "it_ready")
        block = ph.block()

        def par(name, i):
            return k.par[:, bass.ds(i + PAR[name][0], 1)]

        def place(d, n, last=NCH):
            return n if d == 0 else last - 1 - n

        def out(hp, b):
            return k.o_rw[:, bass.ds(hp, 1), b * BANK:(b + 1) * BANK].squeeze(1)

        @block.sync
        def _(sp):
            sp.dma_start(tw[:], d_rw[12]).then_inc(lora_loaded, 16)
            sp.dma_start(al[:], d_rw[13]).then_inc(lora_loaded, 16)
            sp.dma_start(sgl[:], d_rw[14][:, CTX:TOK]).then_inc(lora_loaded, 16)
            sp.wait_ge(lora_loaded, 48)
            sp.wait_ge(zeroed, 2)
            with sp.Fori(0, HP) as hp:
                wait_apart(sp, lora_loaded, hp_loaded, 128 * hp)
                sp.wait_ge(pair_done, hp)
                for n, buf in enumerate((r, kf, v)):
                    sp.dma_start(buf[:], d_rw[hp + HP * n]).then_inc(hp_loaded, 16)
                for d in range(2):
                    for dst, src in ((lw, d_wup), (la, d_aup)):
                        sp.dma_start(dst[d * HD:(d + 1) * HD, d], src[d, :, bass.ds(hp * P, P)]).then_inc(hp_loaded, 16)
                sp.dma_start(gup[:], d_gup[:, bass.ds(hp * P, P)]).then_inc(hp_loaded, 16)
            sp.wait_ge(hp_loaded, 128 * HP)

        @block.gpsimd
        def _(pool):
            for t in (lw, la, arz, ab, kr, small):
                pool.memset(t[:], 0.0).then_inc(zeroed, 1)
            with pool.Fori(0, HP) as hp:
                with pool.Fori(0, NCH) as n:
                    pool.wait_ge(bulk_ready, hp + 1)
                    for d in range(2):
                        c = place(d, n) * CH
                        wait_apart(pool, go, y_ready[d], NCH * hp + n)
                        pool.tensor_copy(bk_s[:, d], bk[:, d, :, bass.ds(c, CH)]).then_inc(staged[d], 1)
                        pool.tensor_copy(ar_s[:, d], ar[:, d, :, bass.ds(c, CH)]).then_inc(staged[d], 1)

        @block.scalar
        def _(act):
            act.wait_ge(lora_loaded, 48)
            act.activation(tw[:], tw[:], ACT.Tanh).then_inc(lora_ready, 1)
            act.activation(sgl[:], sgl[:], ACT.Sigmoid).then_inc(lora_ready, 1)
            with act.Fori(0, HP) as hp:
                wait_apart(act, go, hp_loaded, 128 * (hp + 1))
                for t0, tn in SBLOCKS:
                    act.activation(kk[:, t0:t0 + tn], kf[:, t0:t0 + tn], ACT.Square,
                                   scale=par("k_k", hp)).then_inc(sq_ready, 1)
                for i in range(NZ):
                    (d, b), q = divmod(i // 2, len(BLOCKS)), i % 2
                    t0, tn = BLOCKS[b]
                    wait_apart(act, go, za_ready, NZ * hp + i + 1)
                    act.activation((ar, bk)[q][:, d, 0, t0:t0 + tn], ps[:, 3 + i % 5, 0:tn], ACT.Sigmoid,
                                   bias=par(("w0", "a0")[q], hp + HP * d)).then_inc(za_evicted, 1)
                for b, (t0, tn) in enumerate(SBLOCKS):
                    act.wait_ge(kk_inv, len(SBLOCKS) * hp + b + 1)
                    act.activation(kk[:, t0:t0 + tn], kk[:, t0:t0 + tn], ACT.Sqrt).then_inc(kk_rstd, 1)
                for b in range(3):
                    act.wait_ge(vt_ready, 3 * hp + b + 1)
                    act.copy(vtok[:, 4 * b:4 * b + 4], ps[:, 5 + b].rearrange("p (c f) -> p c f", f=CH)).then_inc(vt_copied, 1)
                for d in range(2):
                    act.wait_ge(log_ready, 4 * hp + 2 * (d + 1))
                    act.activation(e[:], ar[:, d, 1], ACT.Exp, scale=KAPPA).then_inc(e_ready, 1)
                    act.activation(ar[:, d, 0], ar[:, d, 0], ACT.Exp, scale=-KAPPA)
                    act.activation(small[:, d, 3], small[:, d, 2], ACT.Exp, scale=-KAPPA)
                    act.activation(ar[:, d, 1], ar[:, d, 1], ACT.Exp, scale=-KAPPA).then_inc(ar_ready, 1)
                with act.Fori(0, NCH) as n:
                    act.wait_ge(bulk_ready, hp + 1)
                    step = NCH * hp + n
                    for d in range(2):
                        c = place(d, n) * CH
                        wait_apart(act, go, m_ready[d], 2 * step)
                        for h in range(2):
                            rows = slice(h * HD, (h + 1) * HD)
                            act.copy(arz[rows, d, h], ar[rows, d, :, bass.ds(c, CH)]).then_inc(arz_ready[d], 1)
                    for d in range(2):
                        act.wait_ge(tr_ready[d], step + 1)
                        act.copy(flat(bket[:, d]), bank(d, 2)[:, 0:2 * CH]).then_inc(tr_copied[d], 1)
                    for d in range(2):
                        act.wait_ge(masked[d], 2 * step + 1)
                        act.copy(atr[:, d], ab[:, d, :, 0]).then_inc(at_ready[d], 1)
                    for l in range(LEVELS):
                        for d in range(2):
                            if l:
                                act.wait_ge(t_ready[d], TS * step + 2 * l)
                                act.copy(flat(tb[:, d]), bank(d, 0)[:, 0:2 * CH]).then_inc(t_copied[d], 1)
                            act.wait_ge(t_ready[d], TS * step + 2 * l + 1)
                            act.copy(flat(ttb[:, d]), bank(d, 1)[:, 0:2 * CH]).then_inc(t_copied[d], 1)
                    for d in range(2):
                        act.wait_ge(w_ready[d], step + 1)
                        act.copy(wsb[:, d], bank(d, 3)[:, 0:CH]).then_inc(w_copied[d], 1)
                    for d in range(2):
                        act.wait_ge(u_ready[d], step + 1)
                        act.copy(usb[:, d], bank(d, 0)[:, 0:CH]).then_inc(u_copied[d], 1)
                act.wait_ge(centred, hp + 1)
                act.activation(e[:, 0:SEQ], kk[:, CTX:TOK], ACT.Square).then_inc(gn_sq, 1)
                act.wait_ge(gn_inv, hp + 1)
                act.activation(stat[:, 3], stat[:, 2], ACT.Sqrt).then_inc(gn_rstd, 1)
                for b in range(2):
                    wait_apart(act, go, ln_ps, 2 * hp + b + 1)
                    act.activation(e[:, b * BANK:(b + 1) * BANK], ps[:, b], ACT.Identity, bias=par("ln_b", hp),
                                   scale=par("ln_w", hp)).then_inc(ln_done, 1)

        @block.vector
        def _(dve):
            ka0 = PAR["k_a"][0]
            dve.tensor_scalar(rest[:], k.par[:, ka0:ka0 + HP], -1.0, 1.0, ALU.mult, ALU.add).then_inc(go, 1)
            dve.wait_ge(go, 1)
            dve.wait_ge(zeroed, 6)
            dve.wait_ge(lora_ready, 2)
            with dve.Fori(0, HP) as hp:
                c = Chain(dve, dve_step, DVE_PER_PAIR * hp)
                done, wait = c.done, c.wait
                dve.wait_ge(hp_loaded, 128 * (hp + 1))
                for b, (t0, tn) in enumerate(SBLOCKS):
                    dve.wait_ge(kk_sum, len(SBLOCKS) * hp + b + 1)
                    done(dve.tensor_scalar(kk[:, t0:t0 + tn], ps[:, b, 0:tn], 1e-12, None, ALU.max))
                for b, (t0, tn) in enumerate(SBLOCKS):
                    wait(b + 1)
                    dve.reciprocal(kk[:, t0:t0 + tn], kk[:, t0:t0 + tn]).then_inc(kk_inv, 1)
                dve.wait_ge(kk_rstd, len(SBLOCKS) * (hp + 1))
                done(dve.scalar_tensor_tensor(out=kk[:], in0=kf[:], scalar=par("k_k", hp), in1=kk[:], op0=ALU.mult,
                                              op1=ALU.mult))
                dve.wait_ge(za_evicted, NZ * (hp + 1))
                for d in range(2):
                    done(dve.tensor_scalar(bk[:, d, 1], bk[:, d, 0], par("k_a", hp), rest[:, bass.ds(hp, 1)], ALU.mult,
                                           ALU.add))
                wait()
                for d in range(2):
                    done(dve.tensor_tensor(bk[:, d, 1], bk[:, d, 1], kf[:, OFF[d]:OFF[d] + L], ALU.mult))
                for d in range(2):
                    done(dve.scalar_tensor_tensor(out=bk[:, d, 0], in0=kk[:, OFF[d]:OFF[d] + L], scalar=-1.0,
                                                  in1=bk[:, d, 0], op0=ALU.mult, op1=ALU.mult))
                wait()
                done(dve.tensor_tensor(e[:, 0:SEQ], bk[:, 0, 1, CTX:CTX + SEQ], bk[:, 1, 1, 0:SEQ], ALU.add))
                wait()
                dve.scalar_tensor_tensor(out=e[:, 0:SEQ], in0=e[:, 0:SEQ], scalar=par("r_k", hp), in1=r[:, CTX:TOK],
                                         op0=ALU.mult, op1=ALU.mult).then_inc(bonus_in, 1)
                for b in range(2):
                    dve.wait_ge(bonus_ps, 2 * hp + b + 1)
                    done(dve.tensor_tensor(out(hp, b), ps[:, b], v[:, CTX + b * BANK:CTX + (b + 1) * BANK], ALU.mult))
                for d in range(2):
                    done(dve.memset(e[:], 1.0))
                    wait()
                    done(dve.memset(e[:].rearrange("p (c t) -> p c t", t=CH)[:, :, END[1 - d]], 0.0))
                    wait()
                    walk = slice(None, None, (1, -1)[d])
                    done(dve.tensor_tensor_scan(ar[:, d, 1, walk], e[:, walk], ar[:, d, 0, walk], 0.0, ALU.mult, ALU.add))
                    wait()
                    cs = ar[:, d, 1].rearrange("p (c t) -> p c t", t=CH)
                    done(dve.tensor_copy(small[:, d, 0], cs[:, :, MID[d]]))
                    done(dve.tensor_copy(small[:, d, 1], cs[:, :, END[d]]))
                    wait()
                    done(dve.tensor_tensor(cs, cs, small[:, d, 0].unsqueeze(2).to_broadcast([P, NCH, CH]), ALU.subtract))
                    done(dve.tensor_tensor(small[:, d, 2], small[:, d, 1], small[:, d, 0], ALU.subtract))
                    wait()
                    here, there = ((slice(0, NCH - 1), slice(1, NCH)), (slice(1, NCH), slice(0, NCH - 1)))[d]
                    dve.tensor_tensor(small[:, d, 2, here], small[:, d, 2, here], small[:, d, 0, there],
                                      ALU.add).then_inc(log_ready, 1)
                    dve.tensor_tensor(ar[:, d, 0], ar[:, d, 1], ar[:, d, 0], ALU.subtract).then_inc(log_ready, 1)
                    dve.wait_ge(e_ready, 2 * hp + d + 1)
                    done(dve.tensor_tensor(bk[:, d], bk[:, d], e[:].unsqueeze(1).to_broadcast([P, 2, L]), ALU.mult))
                    dve.wait_ge(ar_ready, 2 * hp + d + 1)
                    done(dve.tensor_tensor(ar[:, d, 0], ar[:, d, 0], kk[:, OFF[d]:OFF[d] + L], ALU.mult))
                    done(dve.tensor_tensor(ar[:, d, 1], ar[:, d, 1], r[:, OFF[d]:OFF[d] + L], ALU.mult))
                    wait()
                for d in range(2):
                    done(dve.memset(sbd[:, d], 0.0))
                dve.wait_ge(vt_copied, 3 * (hp + 1))
                wait()
                dve.memset(kk[:], 0.0).then_inc(bulk_ready, 1)

                with dve.Fori(0, NCH) as n:
                    step = NCH * hp + n
                    dve.wait_ge(bulk_ready, hp + 1)
                    for d in range(2):
                        wait_apart(dve, go, tr_ready[d], step)
                        dve.wait_ge(staged[d], 2 * step + 1)
                        dve.tensor_scalar(bke[:, d], bk_s[:, d], small[:, d, 3, bass.ds(place(d, n), 1)], None,
                                          ALU.mult).then_inc(bke_ready[d], 1)
                    for i, dst in enumerate((ab, kr)):
                        for d in range(2):
                            wait_apart(dve, go, m_ready[d], 2 * step + i + 1)
                            dve.copy_predicated(dst[:, d].rearrange("p h i t -> p (h i t)"),
                                                k.keep[:, d].rearrange("p h i t -> p (h i t)"),
                                                bank(d, i)).then_inc(masked[d], 1)
                    for l in range(LEVELS):
                        for d in range(2):
                            dve.wait_ge(p_ready[d], LEVELS * step + l + 1)
                            dve.tensor_tensor(pl[:, d, l % 2], bank(d, 2)[:, 0:2 * CH].rearrange("p (h t) -> p h t", h=2),
                                              k.level[:, d, l].unsqueeze(1).to_broadcast([P, 2, CH]),
                                              ALU.mult).then_inc(pl_ready[d], 1)
                    for d in range(2):
                        dve.wait_ge(t_copied[d], TS * (step + 1) - 1)
                        dve.tensor_tensor(it[:, d], k.ident[:].unsqueeze(1).to_broadcast([P, 2, CH]),
                                          tb[:, d].bitcast(F32), ALU.subtract).then_inc(it_ready[d], 1)
                    for d in range(2):
                        dve.wait_ge(it_ready[d], step + 1)
                        dve.wait_ge(g_ready[d], step + 1)
                        dve.tensor_tensor(flat(er[:, d]), bank(d, 2)[:, 0:2 * CH], flat(it[:, d]),
                                          ALU.add).then_inc(er_ready[d], 1)
                    for d in range(2):
                        dve.wait_ge(n_ready[d], step + 1)
                        dve.tensor_tensor(flat(ttf[:, d]), bank(d, 1)[:, 0:2 * CH], flat(ttb[:, d]).bitcast(F32),
                                          ALU.add).then_inc(ttf_ready[d], 1)
                    for d in range(2):
                        dve.wait_ge(st_ready[d], step + 1)
                        for h in range(2):
                            a, b = h * HD, (h + 1) * HD
                            dve.scalar_tensor_tensor(out=sbd[a:b, d, a:b], in0=sbd[a:b, d, a:b],
                                                     scalar=small[a:b, d, 3, bass.ds(place(d, n), 1)],
                                                     in1=bank(d, 3)[a:b, a:b], op0=ALU.mult,
                                                     op1=ALU.add).then_inc(st_done[d], 1)
                    for d in range(2):
                        wait_apart(dve, go, y_added[1 - d], step + d)
                        dve.wait_ge(y_ready[d], step + 1)
                        yt = ytok[:, bass.ds(place(d, n, SC), 1)].squeeze(1)
                        dve.tensor_tensor(yt, yt, bank(d, 2)[:, 0:CH], ALU.add).then_inc(y_added[d], 1)

                G = 2 * SEQ // P
                y = kk[:, CTX:TOK].rearrange("p (g f) -> p g f", f=HD)
                for d in range(2):
                    dve.wait_ge(y_added[d], NCH * (hp + 1))
                done(dve.tensor_reduce(stat[:, 0], y, AX.X, ALU.add))
                wait()
                done(dve.tensor_scalar(stat[:, 1], stat[:, 0], 1.0 / HD, None, ALU.mult))
                wait()
                dve.tensor_tensor(y, y, stat[:, 1].unsqueeze(2).to_broadcast([P, G, HD]), ALU.subtract).then_inc(centred, 1)
                dve.wait_ge(gn_sq, hp + 1)
                done(dve.tensor_reduce(stat[:, 0], e[:, 0:SEQ].rearrange("p (g f) -> p g f", f=HD), AX.X, ALU.add))
                wait()
                done(dve.tensor_scalar(stat[:, 1], stat[:, 0], 1.0 / HD, GN_EPS, ALU.mult, ALU.add))
                wait()
                dve.reciprocal(stat[:, 2], stat[:, 1]).then_inc(gn_inv, 1)
                dve.wait_ge(gn_rstd, hp + 1)
                dve.tensor_tensor(y, y, stat[:, 3].unsqueeze(2).to_broadcast([P, G, HD]), ALU.mult).then_inc(normed, 1)
                for b in range(2):
                    dve.wait_ge(ln_done, 2 * hp + b + 1)
                    eb = e[:, b * BANK:(b + 1) * BANK]
                    done(dve.tensor_tensor(eb, eb, out(hp, b), ALU.add))
                    dve.wait_ge(gate_ps, 2 * hp + b + 1)
                    wait()
                    ins = dve.tensor_tensor(out(hp, b), eb, ps[:, 2 + b], ALU.mult)
                    if b == 0:
                        done(ins)
                ins.then_inc(pair_done, 1)
                assert c.n == DVE_PER_PAIR, c.n

        @block.tensor
        def _(pe):
            pe.wait_ge(go, 1)
            pe.wait_ge(lora_ready, 2)
            pe.wait_ge(zeroed, 6)
            with pe.Fori(0, HP) as hp:
                pe.wait_ge(pair_done, hp)
                pe.wait_ge(hp_loaded, 128 * (hp + 1))
                for b, (t0, tn) in enumerate(SBLOCKS):
                    pe.wait_ge(sq_ready, len(SBLOCKS) * hp + b + 1)
                    pe.matmul(ps[:, b, 0:tn], k.same64[:], kk[:, t0:t0 + tn], start=True, stop=True).then_inc(kk_sum, 1)
                for i in range(NZ):
                    (d, b), q = divmod(i // 2, len(BLOCKS)), i % 2
                    t0, tn = BLOCKS[b]
                    pe.wait_ge(za_evicted, NZ * hp + max(i - 4, 0))
                    src = (tw, al)[q][:, OFF[d] + t0:OFF[d] + t0 + tn]
                    pe.matmul(ps[:, 3 + i % 5, 0:tn], (lw, la)[q][:, d], src, start=True, stop=True).then_inc(za_ready, 1)
                pe.wait_ge(za_evicted, NZ * (hp + 1))
                for b in range(3):
                    for j in range(4):
                        c = 4 * b + j
                        mm = pe.transpose(ps[:, 5 + b, j * CH:(j + 1) * CH], v[:, c * CH:(c + 1) * CH], k.ident[:])
                    mm.then_inc(vt_ready, 1)
                pe.wait_ge(bonus_in, hp + 1)
                for b in range(2):
                    pe.matmul(ps[:, b], k.same64[:], e[:, b * BANK:(b + 1) * BANK], start=True,
                              stop=True).then_inc(bonus_ps, 1)
                with pe.Fori(0, NCH) as n:
                    pe.wait_ge(bulk_ready, hp + 1)
                    step = NCH * hp + n
                    vt = [vtok[:, bass.ds(place(d, n, SC), 1)].squeeze(1) for d in range(2)]
                    for d in range(2):
                        pe.wait_ge(staged[d], 2 * (step + 1))
                        pe.wait_ge(arz_ready[d], 2 * (step + 1))
                        pe.wait_ge(u_copied[d], step)
                        pe.wait_ge(ttf_ready[d], step)
                        for i in range(2):
                            pe.matmul(bank(d, i), bk_s[:, d, i], arz[:, d].rearrange("p h i t -> p (h i t)"), start=True,
                                      stop=True).then_inc(m_ready[d], 1)
                    for d in range(2):
                        pe.wait_ge(y_added[d], step)
                        pe.wait_ge(bke_ready[d], step + 1)
                        for i in range(2):
                            mm = pe.transpose(bank(d, 2)[:, i * CH:(i + 1) * CH], bke[:, d, i], k.ident[:])
                        mm.then_inc(tr_ready[d], 1)
                    for l in range(LEVELS):
                        for d in range(2):
                            if l == 0:
                                pe.wait_ge(tr_copied[d], step + 1)
                                pe.wait_ge(at_ready[d], step + 1)
                            else:
                                pe.wait_ge(pl_ready[d], LEVELS * step + l)
                                if l >= 2:
                                    pe.wait_ge(t_copied[d], TS * step + 2 * (l - 1))
                            for h in range(2):
                                t_inv = k.identr[:] if l == 0 else pl[:, d, 0, h] if l == 1 else tb[:, d, h]
                                at = bank(d, 2)[:, h * CH:(h + 1) * CH]
                                pe.matmul(at, k.identr[:], k.identr[:], start=True, stop=False)
                                mm = pe.matmul(at, atr[:, d, h], t_inv, start=False, stop=True)
                            mm.then_inc(p_ready[d], 1)
                        for d in range(2):
                            pe.wait_ge(pl_ready[d], LEVELS * step + l + 1)
                            if l:
                                pe.wait_ge(t_copied[d], TS * step + 2 * l - 1)
                                for h in range(2):
                                    mm = pe.matmul(bank(d, 0)[:, h * CH:(h + 1) * CH], ttb[:, d, h], pl[:, d, l % 2, h],
                                                   start=True, stop=True)
                                mm.then_inc(t_ready[d], 1)
                            else:
                                pe.wait_ge(masked[d], 2 * (step + 1))
                            for h in range(2):
                                mm = pe.matmul(bank(d, 1)[:, h * CH:(h + 1) * CH], pl[:, d, l % 2, h],
                                               ttb[:, d, h] if l else k.identr[:], start=True, stop=True)
                            mm.then_inc(t_ready[d], 1)
                    for d in range(2):
                        pe.wait_ge(t_copied[d], TS * (step + 1) - 1)
                        for h in range(2):
                            mm = pe.matmul(bank(d, 2)[:, h * CH:(h + 1) * CH], ab[:, d, h, 0], tb[:, d, h].bitcast(F32),
                                           start=True, stop=True)
                        mm.then_inc(g_ready[d], 1)
                    for d in range(2):
                        pe.wait_ge(st_done[d], 2 * step)
                        for h in range(2):
                            a, b = h * HD, (h + 1) * HD
                            pe.matmul(bank(d, 3)[:, a:b], ar_s[:, d, 0], sbd[:, d, a:b], start=True, stop=False)
                            mm = pe.matmul(bank(d, 3)[:, a:b], kr[:, d, h, 0], vt[d][:, a:b], start=False, stop=True)
                        mm.then_inc(w_ready[d], 1)
                    for d in range(2):
                        pe.wait_ge(er_ready[d], step + 1)
                        pe.wait_ge(t_copied[d], TS * (step + 1))
                        for h in range(2):
                            mm = pe.matmul(bank(d, 1)[:, h * CH:(h + 1) * CH], er[:, d, h], ttb[:, d, h], start=True,
                                           stop=True)
                        mm.then_inc(n_ready[d], 1)
                    for d in range(2):
                        pe.wait_ge(ttf_ready[d], step + 1)
                        pe.wait_ge(w_copied[d], step + 1)
                        for h in range(2):
                            a, b = h * HD, (h + 1) * HD
                            mm = pe.matmul(bank(d, 0)[:, a:b], ttf[:, d, h], wsb[:, d, a:b], start=True, stop=True)
                        mm.then_inc(u_ready[d], 1)
                    for d in range(2):
                        pe.wait_ge(u_copied[d], step + 1)
                        for h in range(2):
                            a, b = h * HD, (h + 1) * HD
                            pe.matmul(bank(d, 2)[:, a:b], ar_s[:, d, 1], sbd[:, d, a:b], start=True, stop=False)
                            pe.matmul(bank(d, 2)[:, a:b], ab[:, d, h, 1], usb[:, d, a:b], start=False, stop=False)
                            mm = pe.matmul(bank(d, 2)[:, a:b], kr[:, d, h, 1], vt[d][:, a:b], start=False, stop=True)
                        mm.then_inc(y_ready[d], 1)
                    for d in range(2):
                        pe.matmul(bank(d, 3)[:, 0:P], bket[:, d, 0], usb[:, d], start=True, stop=False)
                        pe.matmul(bank(d, 3)[:, 0:P], bket[:, d, 1], vt[d], start=False, stop=True).then_inc(st_ready[d], 1)
                pe.wait_ge(normed, hp + 1)
                for b in range(2):
                    for j in range(4):
                        c = CTX // CH + 4 * b + j
                        mm = pe.transpose(ps[:, b, j * CH:(j + 1) * CH], kk[:, c * CH:(c + 1) * CH], k.ident[:])
                    mm.then_inc(ln_ps, 1)
                for b in range(2):
                    pe.matmul(ps[:, 2 + b], gup[:], sgl[:, b * BANK:(b + 1) * BANK], start=True,
                              stop=True).then_inc(gate_ps, 1)




def merge(nc, k, hi, lo, d_w, d_gate):
    NB = SEQ // BANK
    ROUNDS = KT // 2
    U = 2 * NB
    gates = d_gate.rearrange("(h t) p n -> t p h n", h=2)
    parts = [k.o_na[:, t] for t in range(HP)] + [k.o_rw[:, t] for t in range(HP)]
    with Phase(nc, "mg") as ph:
        raw = ph.sb("w_raw", [P, 2, KT, P])
        wh, wl = ph.sb("w_hi", [P, 2, KT, P], F32R), ph.sb("w_lo", [P, 2, KT, P], F32R)
        oh = ph.sb("o_hi", [P, KT, SEQ], F32R)
        g = ph.sb("gates", [P, 2, 2, BANK])
        m = ph.sb("gated", [P, 2, BANK])
        whole = ph.sb("whole", [P, 2, BANK])
        ps = ph.psum(8)
        w_loaded = [ph.sem(f"w_loaded{s}") for s in range(2)]
        g_loaded = [ph.sem(f"g_loaded{s}") for s in range(2)]
        o_hi_done, o_lo_done, w_hi_done, w_lo_done, out_ready, gated, whole_ready, m_hi_done, m_lo_done = ph.sems(
            "o_hi_done o_lo_done w_hi_done w_lo_done out_ready gated whole_ready m_hi_done m_lo_done")
        block = ph.block()

        @block.sync
        def _(sp):
            with sp.Fori(0, ROUNDS) as i:
                for s in range(2):
                    sp.wait_ge(w_lo_done, 2 * i)
                    sp.dma_start(raw[:, s], d_w[2 * i + s]).then_inc(w_loaded[s], 16)
                for u in range(U):
                    s, b = divmod(u, NB)
                    sp.wait_ge(gated, 2 * (U * i + max(u - 1, 0)) if u else 2 * U * i)
                    sp.dma_start(g[:, u % 2], gates[2 * i + s][:, :, b * BANK:(b + 1) * BANK]).then_inc(g_loaded[u % 2], 16)

        @block.scalar
        def _(act):
            for t in range(KT):
                act.copy(oh[:, t], parts[t]).then_inc(o_hi_done, 1)
            with act.Fori(0, ROUNDS) as i:
                for s in range(2):
                    act.wait_ge(out_ready, U * i)
                    act.wait_ge(w_loaded[s], 16 * (i + 1))
                    act.copy(wh[:, s], raw[:, s]).then_inc(w_hi_done, 1)
                for u in range(U):
                    s, b = divmod(u, NB)
                    wait_apart(act, o_hi_done, whole_ready, U * i + u + 1)
                    act.copy(hi[:, bass.ds(2 * i + s, 1), b * BANK:(b + 1) * BANK].squeeze(1),
                             whole[:, u % 2]).then_inc(m_hi_done, 1)

        @block.vector
        def _(dve):
            for t in range(KT):
                dve.wait_ge(o_hi_done, t + 1)
                dve.tensor_tensor(parts[t].bitcast(F32R), parts[t], oh[:, t].bitcast(F32),
                                  ALU.subtract).then_inc(o_lo_done, 1)

            def split_lo(i, u):
                s, b = divmod(u, NB)
                at = (slice(None), bass.ds(2 * i + s, 1), slice(b * BANK, (b + 1) * BANK))
                dve.wait_ge(m_hi_done, U * i + u + 1)
                dve.tensor_tensor(lo[at].squeeze(1), whole[:, u % 2], hi[at].squeeze(1).bitcast(F32),
                                  ALU.subtract).then_inc(m_lo_done, 1)

            with dve.Fori(0, ROUNDS) as i:
                for s in range(2):
                    dve.wait_ge(w_hi_done, 2 * i + s + 1)
                    dve.tensor_tensor(wl[:, s], raw[:, s], wh[:, s].bitcast(F32), ALU.subtract).then_inc(w_lo_done, 1)
                for u in range(U):
                    done = U * i + u
                    dve.wait_ge(out_ready, done + 1)
                    dve.wait_ge(g_loaded[u % 2], 16 * (NB * i + u // 2 + 1))
                    if u >= 2:
                        dve.wait_ge(m_lo_done, done - 1)
                    for h, dst in enumerate((m, whole)):
                        dve.tensor_tensor(dst[:, u % 2], ps[:, 2 * u + h], g[:, u % 2, h], ALU.mult).then_inc(gated, 1)
                    dve.wait_ge(gated, 2 * (done + 1))
                    dve.tensor_tensor(whole[:, u % 2], whole[:, u % 2], m[:, u % 2], ALU.add).then_inc(whole_ready, 1)
                    if u:
                        split_lo(i, u - 1)
                split_lo(i, U - 1)

        @block.tensor
        def _(pe):
            pe.wait_ge(o_lo_done, KT)
            with pe.Fori(0, ROUNDS) as i:
                for u in range(U):
                    s, b = divmod(u, NB)
                    pe.wait_ge(w_lo_done, 2 * i + s + 1)
                    pe.wait_ge(gated, 2 * U * i)
                    for h in range(2):
                        for kt in range(HP * h, HP * (h + 1)):
                            tok = slice(b * BANK, (b + 1) * BANK)
                            mm = three(pe, ps[:, 2 * u + h], wh[:, s, kt], wl[:, s, kt], oh[:, kt, tok],
                                       parts[kt].bitcast(F32R)[:, tok], kt == HP * h, kt == HP * (h + 1) - 1)
                    mm.then_inc(out_ready, 1)


def hybrid_layer(nc, par, x, ctx, w_ada, w_ffn1, w_ffn2, w_q, w_k, w_v, w_rw, w_gate, rpb, w_up, a_up, g_up,
                 w_merge, w_out, out):
    k = Kept()
    k.d_par, k.d_x, k.d_ctx, k.d_w_ada = par, x, ctx, w_ada
    d_q = nc.dram_tensor("q_scratch", (HP, P, SEQ), F32).ap()
    d_k = nc.dram_tensor("k_scratch", (HP, P, TOK), F32).ap()
    d_v = nc.dram_tensor("v_scratch", (TOK // P, P, HEADS * HD), F32).ap()
    d_rw = nc.dram_tensor("rw_scratch", (RW_TILES, P, STREAM), F32).ap()
    d_gate = nc.dram_tensor("gate_scratch", (2 * KT, P, SEQ), F32).ap()
    table = (2 * WIN_H + 1) * RPB_ROW
    k.d_rpb_source = bass.AP(tensor=rpb.tensor, offset=0, ap=[[table, HEADS], [0, GRID_W], [1, table]])
    k.d_rpb_copies = nc.dram_tensor("rpb_scratch", (HEADS, GRID_W, table), F32).ap()
    d_rpb = bass.AP(tensor=k.d_rpb_copies.tensor, offset=GRID_W - 1,
                    ap=[[GRID_W * table, HEADS], [table - 1, GRID_W], [RPB_ROW, 2 * WIN_H + 1], [1, GRID_W]])

    def sb(stack, name, shape, dtype=F32):
        return stack.enter_context(nc.sbuf_tensor(name, shape, dtype))

    with ExitStack() as whole:
        k.par = sb(whole, "params", [P, PAR_COLS])
        k.x = sb(whole, "x", [P, KT, SEQ])
        k.ones = sb(whole, "ones", [P, P])
        k.ident, k.identr = sb(whole, "ident", [P, P]), sb(whole, "ident_r", [P, P], F32R)
        k.mod = sb(whole, "mod", [P, NMOD * KT, 2])
        k.gain, k.gate = sb(whole, "gain", [P, 3, 2, KT]), sb(whole, "gate", [P, 3, 2, KT])

        with ExitStack() as front:
            k.ctx = sb(front, "context", [P, KT, CTX])
            load_constants(nc, k)
            modulation(nc, k)
            hi, lo = sb(front, "h_hi", [P, KT, SEQ], F32R), sb(front, "h_lo", [P, KT, SEQ], F32R)
            norm(nc, k, "norm1", k.x, SEQ, 0, 0, hi, lo)
            swiglu(nc, k, "ffn1", k.x, SEQ, 0, 0, hi, lo, w_ffn1)
            norm(nc, k, "norm1c", k.ctx, CTX, 0, 1, hi, lo)
            swiglu(nc, k, "ffn1c", k.ctx, CTX, 0, 1, hi, lo, w_ffn1)

            hic, loc = sb(front, "hc_hi", [P, KT, CTX], F32R), sb(front, "hc_lo", [P, KT, CTX], F32R)
            norm(nc, k, "norm2", k.x, SEQ, 1, 0, hi, lo)
            norm(nc, k, "norm2c", k.ctx, CTX, 1, 1, hic, loc)
            latents = [(hi[:, :, a:a + n], lo[:, :, a:a + n], n) for a, n in halves(SEQ)]
            both = latents + [(hic[:], loc[:], CTX)]
            project(nc, k, "pk", HP, w_k, both, "scale", d_k, 1.0)
            project(nc, k, "prw", RW_TILES, w_rw, both, "shift", d_rw)
            project(nc, k, "pq", HP, w_q, latents, "scale", d_q, HD ** -0.5)
            project(nc, k, "pg", 2 * KT, w_gate, latents, "gate", d_gate, PAR["b_gate"][0])
            project_v(nc, k, hi, lo, hic, loc, w_v, d_v)

        with ExitStack() as mix:
            k.o_rw = sb(mix, "o_rw", [P, HP, SEQ])
            with ExitStack() as masks:
                k.same64 = sb(masks, "same_head", [P, P])
                k.keep = sb(masks, "keep", [P, 2, 2, 2, CH], U8)
                k.level = sb(masks, "level", [P, 2, LEVELS, CH])
                rwkv_masks(nc, k)
                rwkv(nc, k, d_rw, w_up, a_up, g_up)
            k.o_na = sb(mix, "o_na", [P, HP, SEQ])
            attention(nc, k, d_q, d_k, d_v, d_rpb)
            hi, lo = sb(mix, "m_hi", [P, KT, SEQ], F32R), sb(mix, "m_lo", [P, KT, SEQ], F32R)
            merge(nc, k, hi, lo, w_merge, d_gate)
            merged = [(hi[:, :, a:a + n], lo[:, :, a:a + n], n) for a, n in halves(SEQ)]
            project(nc, k, "po", KT, w_out, merged, "residual")

        with ExitStack() as back:
            hi, lo = sb(back, "h2_hi", [P, KT, SEQ], F32R), sb(back, "h2_lo", [P, KT, SEQ], F32R)
            norm(nc, k, "norm3", k.x, SEQ, 2, 0, hi, lo)
            swiglu(nc, k, "ffn2", k.x, SEQ, 2, 0, hi, lo, w_ffn2)
            norm(nc, k, "norm4", k.x, SEQ, d_out=out)


def pieces(w):
    rows, cols = w.shape
    return w.reshape(rows // P, P, cols // P, P).transpose(2, 1, 0, 3)


def ffn_pieces(wg, wu, wd):
    g, u = pieces(wg), pieces(wu)
    d = wd.reshape(FT, P, KT, P)
    return np.stack([g[0::2], u[0::2], g[1::2], u[1::2], d[0::2], d[1::2]], 1).reshape(3 * FT, P, KT, P)


def feature_tiles(a):
    return a.T.reshape(-1, P, a.shape[0]).transpose(1, 0, 2)


def layout(a):
    w, mu = a["w_in"][0], a["rw_mu"][0]
    NA, RW = HEADS * HD, RW_TILES * P
    vectors = [a["c"], a["c_ctx"], a["b_ada"], a["norm_ffn1"], a["norm_mix"], a["norm_ffn2"], a["norm_final"],
               a["b_gate"], mu[0], mu[1], a["rw_w0"], a["rw_a0"], a["rw_k_k"], a["rw_k_a"], a["rw_r_k"],
               a["rw_ln_w"], a["rw_ln_b"]]
    rpb = np.zeros((HEADS, 2 * WIN_H + 1, RPB_ROW), np.float32)
    left = GRID_W - WIN_W
    rpb[:, 1:2 * WIN_H, left:left + 2 * WIN_W - 1] = a["na_rpb"][0]
    return {
        "par": np.concatenate([v.reshape(-1, P).T for v in vectors], 1),
        "x": feature_tiles(a["x"][0]),
        "ctx": feature_tiles(a["ctx"][0]),
        "w_ada": a["w_ada"][0].reshape(KT, P, NMOD * KT // 4, 4, P).transpose(2, 1, 3, 0, 4),
        "w_ffn1": ffn_pieces(a["ffn1_wg"][0], a["ffn1_wu"][0], a["ffn1_wd"][0]),
        "w_ffn2": ffn_pieces(a["ffn2_wg"][0], a["ffn2_wu"][0], a["ffn2_wd"][0]),
        "w_q": pieces(w[:, 0:NA]),
        "w_k": pieces(w[:, NA:2 * NA]),
        "w_v": w[:, 2 * NA:3 * NA].reshape(KT, P, NA).transpose(1, 0, 2),
        "w_rw": pieces(w[:, 3 * NA:3 * NA + RW]),
        "w_gate": pieces(w[:, 3 * NA + RW:]),
        "rpb": rpb,
        "w_up": a["rw_w_up"][0],
        "a_up": a["rw_a_up"][0],
        "g_up": a["rw_g_up"][0],
        "w_merge": pieces(np.concatenate([a["p_na"][0], a["p_rw"][0]])),
        "w_out": pieces(a["w_out"][0]),
    }


def kernel(**inputs):
    import concourse.bacc as _bacc
    from concourse.bass_utils import run_bass_kernel_spmd as _run

    nc = _bacc.Bacc("TRN2", target_bir_lowering=False, num_devices=1)
    arrays, args = {}, {}
    for name, a in layout({name: np.asarray(a) for name, a in inputs.items()}).items():
        a = np.ascontiguousarray(a)
        arrays[f"in_{name}_dram"] = a
        args[name] = nc.dram_tensor(f"in_{name}_dram", a.shape, F32, kind="ExternalInput").ap()
    out = nc.dram_tensor("out_0_dram", (P, KT, SEQ), F32, kind="ExternalOutput").ap()
    hybrid_layer(nc, out=out, **args)
    r = _run(nc, [arrays], core_ids=[0])
    return r.results[0]["out_0_dram"].transpose(2, 1, 0).reshape(1, SEQ, D)
```

```python
from contextlib import ExitStack

import numpy as np

import concourse.bass as bass
from concourse import mybir

ALU = mybir.AluOpType
ACT = mybir.ActivationFunctionType
AX = mybir.AxisListType
F32 = mybir.dt.float32
F32R = mybir.dt.float32r
U8 = mybir.dt.uint8

P = 128
D = 1024
KT = D // P
SEQ = 1024
CTX = 256
TOK = SEQ + CTX
D_FF = 2816
FT = D_FF // P
GRID_W = 64
ROWS = SEQ // GRID_W
HEADS = 8
HD = 64
HP = HEADS // 2
WIN_H, WIN_W = 8, 16
RPB_ROW = 2 * GRID_W - 1
NMOD = 9
EPS = 1e-6
GN_EPS = 64e-5
KAPPA = 0.6065306597126334
MASKED = -1e30
RW_TILES = 15
BANK = 512
CH = 128
NCH = TOK // CH
STREAM = CTX + SEQ + CTX

PAR = {}
_at = 0
for _name, _n in (("c", KT), ("c_ctx", KT), ("b_ada", NMOD * KT), ("norm_ffn1", KT), ("norm_mix", KT),
                  ("norm_ffn2", KT), ("norm_final", KT), ("b_gate", 2 * KT), ("mu_prev", RW_TILES),
                  ("mu_next", RW_TILES), ("w0", 2 * HP), ("a0", 2 * HP), ("k_k", HP), ("k_a", HP),
                  ("r_k", HP), ("ln_w", HP), ("ln_b", HP)):
    PAR[_name] = (_at, _n)
    _at += _n
PAR_COLS = _at


class Kept:
    pass


class Chain:

    def __init__(self, eng, sem, at=0):
        self.eng, self.sem, self.at, self.n = eng, sem, at, 0

    def done(self, ins):
        ins.then_inc(self.sem, 1)
        self.n += 1
        return self.n

    def wait(self, n=None):
        self.eng.wait_ge(self.sem, self.at + (self.n if n is None else n))


class Phase(ExitStack):
    last = set()

    def __init__(self, nc, tag):
        super().__init__()
        self.nc, self.tag, self.taken = nc, tag, set()

    def __exit__(self, *raised):
        super().__exit__(*raised)
        start = None
        for n in sorted(self.taken):
            if start is None:
                start = n
            if n + 1 not in self.taken:
                self.nc.gpsimd.sem_clear(range(start, n + 1))
                start = None
        Phase.last = self.taken

    def sb(self, name, shape, dtype=F32):
        return self.enter_context(self.nc.sbuf_tensor(f"{self.tag}_{name}", shape, dtype))

    def psum(self, banks):
        return self.enter_context(self.nc.psum_tensor(f"{self.tag}_ps", [P, banks, BANK], F32))

    def sem(self, name):
        sem = self.enter_context(self.nc.semaphore(f"{self.tag}_{name}"))
        assert sem.num not in Phase.last
        self.taken.add(sem.num)
        return sem

    def sems(self, names):
        return [self.sem(name) for name in names.split()]

    def block(self):
        return self.enter_context(self.nc.Block())


def wait_apart(eng, met, sem, value):
    value = eng.to_reg(value)
    eng.wait_ge(met, 1)
    eng.wait_ge(sem, value)


def halves(n):
    return [(a, min(BANK, n - a)) for a in range(0, n, BANK)]


def load_constants(nc, k):
    with Phase(nc, "const") as ph:
        par_loaded, pool_done, ident_ready = ph.sems("par_loaded pool_done ident_ready")
        block = ph.block()

        @block.sync
        def _(sp):
            sp.dma_start(k.par[:], k.d_par).then_inc(par_loaded, 16)
            sp.dma_start(k.x[:], k.d_x).then_inc(par_loaded, 16)
            sp.dma_start(k.ctx[:], k.d_ctx).then_inc(par_loaded, 16)
            sp.wait_ge(par_loaded, 48)

        @block.gpsimd
        def _(pool):
            pool.memset(k.ones[:], 1.0).then_inc(pool_done, 1)
            pool.memset(k.ident[:], 0.0).then_inc(pool_done, 1)
            pool.wait_ge(pool_done, 2)
            pool.affine_select(out=k.ident[:], in_=k.ident[:], compare_op=ALU.not_equal, fill=1.0, base=0,
                               pattern=[[-1, P]], channel_multiplier=1).then_inc(ident_ready, 1)

        @block.scalar
        def _(act):
            act.wait_ge(ident_ready, 1)
            act.copy(k.identr[:], k.ident[:])


def modulation(nc, k):
    COLS = BANK
    TILES = COLS // P
    ROUNDS = NMOD * D // COLS // 2
    with Phase(nc, "ada") as ph:
        w = ph.sb("ada_w", [P, 2, KT, COLS])
        sc = ph.sb("silu_c", [P, KT, P])
        rows = ph.sb("mod_rows", [P, 2, COLS])
        ps = ph.psum(4)
        loaded = [ph.sem(f"ada_loaded{s}") for s in range(2)]
        rows_ready = [ph.sem(f"rows_ready{s}") for s in range(2)]
        zeroed, silu_ready, rows_copied, turned, evicted, mod_ready = ph.sems("zeroed silu_ready rows_copied turned evicted mod_ready")
        block = ph.block()

        @block.sync
        def _(sp):
            with sp.Fori(0, ROUNDS) as i:
                for s in range(2):
                    sp.wait_ge(rows_ready[s], i)
                    sp.dma_start(w[:, s], k.d_w_ada[2 * i + s]).then_inc(loaded[s], 16)

        @block.scalar
        def _(act):
            c0 = PAR["c"][0]
            act.wait_ge(zeroed, 1)
            act.activation(sc[:, :, 0:2].rearrange("p t v -> p v t"), k.par[:, c0:c0 + 2 * KT].rearrange("p (v t) -> p v t", v=2),
                           ACT.Silu).then_inc(silu_ready, 1)
            with act.Fori(0, ROUNDS) as i:
                for s in range(2):
                    act.wait_ge(rows_ready[s], i + 1)
                    act.wait_ge(turned, 2 * i)
                    act.copy(rows[:, s], ps[:, s]).then_inc(rows_copied, 1)

        @block.tensor
        def _(pe):
            pe.wait_ge(silu_ready, 1)
            with pe.Fori(0, ROUNDS) as i:
                for s in range(2):
                    pe.wait_ge(rows_copied, 2 * i)
                    pe.wait_ge(loaded[s], 16 * (i + 1))
                    for kt in range(KT):
                        mm = pe.matmul(ps[:, s], sc[:, kt, :], w[:, s, kt, :], start=kt == 0, stop=kt == KT - 1)
                    mm.then_inc(rows_ready[s], 1)
                for s in range(2):
                    pe.wait_ge(rows_copied, 2 * i + s + 1)
                    pe.wait_ge(evicted, 2 * i)
                    for t in range(TILES):
                        mm = pe.transpose(ps[:, 2 + s, t * P:(t + 1) * P], rows[:, s, t * P:(t + 1) * P], k.ident[:])
                    mm.then_inc(turned, 1)

        @block.vector
        def _(dve):
            b0 = PAR["b_ada"][0]
            dve.memset(sc[:], 0.0).then_inc(zeroed, 1)
            with dve.Fori(0, ROUNDS) as i:
                for s in range(2):
                    first = (2 * i + s) * TILES
                    dve.wait_ge(turned, 2 * i + s + 1)
                    dve.tensor_tensor(k.mod[:, bass.ds(first, TILES), :],
                                      ps[:, 2 + s].rearrange("p (t c) -> p t c", c=P)[:, :, 0:2],
                                      k.par[:, bass.ds(first + b0, TILES)].unsqueeze(2).to_broadcast([P, TILES, 2]),
                                      ALU.add).then_inc(evicted, 1)
            dve.wait_ge(evicted, 2 * ROUNDS)
            for n, (gain, scale, gate, half) in enumerate((("norm_ffn1", 1, 2, 0.5), ("norm_mix", 4, 5, 1.0),
                                                           ("norm_ffn2", 7, 8, 0.5))):
                g0 = PAR[gain][0]
                for v in range(2):
                    dve.scalar_tensor_tensor(out=k.gain[:, n, v, :], in0=k.mod[:, scale * KT:(scale + 1) * KT, v],
                                             scalar=1.0, in1=k.par[:, g0:g0 + KT], op0=ALU.add,
                                             op1=ALU.mult).then_inc(mod_ready, 1)
                    dve.tensor_scalar(k.gate[:, n, v, :], k.mod[:, gate * KT:(gate + 1) * KT, v], half, None,
                                      ALU.mult).then_inc(mod_ready, 1)


def norm(nc, k, tag, x, n, which=None, v=0, hi=None, lo=None, d_out=None):
    blocks = halves(n)
    final = d_out is not None
    with Phase(nc, tag) as ph:
        sq = ph.sb("sq", [P, 2, BANK])
        ms = ph.sb("mean_square", [P, BANK])
        inv = ph.sb("inv_ms", [P, BANK])
        rstd = ph.sb("rstd", [P, 2, BANK])
        xn = ph.sb("x_normed", [P, 2, BANK])
        h = ph.sb("h_whole", [P, 2, BANK])
        ps = ph.psum(2)
        sq_ready, sq_used, ms_ready, inv_ready, rstd_ready, xn_ready, h_ready, lo_ready, stored = ph.sems(
            "sq_ready sq_used ms_ready inv_ready rstd_ready xn_ready h_ready lo_ready stored")
        block = ph.block()

        @block.sync
        def _(sp):
            if final:
                for b, (t0, tn) in enumerate(blocks):
                    for kt in range(KT):
                        sp.wait_ge(xn_ready, b * KT + kt + 1)
                        sp.dma_start(d_out[:, kt, t0:t0 + tn], x[:, kt, t0:t0 + tn]).then_inc(stored, 16)
                sp.wait_ge(stored, 16 * KT * len(blocks))

        @block.scalar
        def _(act):
            for b, (t0, tn) in enumerate(blocks):
                for kt in range(KT):
                    i = b * KT + kt
                    if i >= 2:
                        act.wait_ge(sq_used, i - 1)
                    act.activation(sq[:, i % 2, 0:tn], x[:, kt, t0:t0 + tn], ACT.Square).then_inc(sq_ready, 1)
            for b, (t0, tn) in enumerate(blocks):
                act.wait_ge(inv_ready, b + 1)
                act.activation(rstd[:, b, 0:tn], inv[:, 0:tn], ACT.Sqrt).then_inc(rstd_ready, 1)
            for b, (t0, tn) in enumerate(blocks if not final else ()):
                for kt in range(KT):
                    i = b * KT + kt
                    scale, shift = k.gain[:, which, v, kt:kt + 1], k.mod[:, which * 3 * KT + kt, v:v + 1]
                    act.wait_ge(xn_ready, i + 1)
                    if i >= 2:
                        act.wait_ge(lo_ready, i - 1)
                    act.activation(h[:, i % 2, 0:tn], xn[:, i % 2, 0:tn], ACT.Identity, bias=shift, scale=scale)
                    act.activation(hi[:, kt, t0:t0 + tn], xn[:, i % 2, 0:tn], ACT.Identity, bias=shift,
                                   scale=scale).then_inc(h_ready, 1)

        @block.tensor
        def _(pe):
            for b, (t0, tn) in enumerate(blocks):
                for kt in range(KT):
                    pe.wait_ge(sq_ready, b * KT + kt + 1)
                    mm = pe.matmul(ps[:, b, 0:tn], k.ones[:], sq[:, kt % 2, 0:tn], start=kt == 0, stop=kt == KT - 1)
                    mm.then_inc(sq_used, 1)
        def split_lo(dve, i):
            b, kt = divmod(i, KT)
            t0, tn = blocks[b]
            dve.wait_ge(h_ready, i + 1)
            dve.tensor_tensor(lo[:, kt, t0:t0 + tn], h[:, i % 2, 0:tn], hi[:, kt, t0:t0 + tn].bitcast(F32),
                              ALU.subtract).then_inc(lo_ready, 1)

        @block.vector
        def _(dve):
            for b, (t0, tn) in enumerate(blocks):
                dve.wait_ge(sq_used, (b + 1) * KT)
                if b:
                    dve.wait_ge(inv_ready, b)
                dve.tensor_scalar(ms[:, 0:tn], ps[:, b, 0:tn], 1.0 / D, EPS, ALU.mult, ALU.add).then_inc(ms_ready, 1)
                dve.wait_ge(ms_ready, b + 1)
                if b:
                    dve.wait_ge(rstd_ready, b)
                dve.reciprocal(inv[:, 0:tn], ms[:, 0:tn]).then_inc(inv_ready, 1)
            for b, (t0, tn) in enumerate(blocks):
                dve.wait_ge(rstd_ready, b + 1)
                for kt in range(KT):
                    i = b * KT + kt
                    if final:
                        xs, g = x[:, kt, t0:t0 + tn], PAR["norm_final"][0] + kt
                        dve.scalar_tensor_tensor(out=xs, in0=xs, scalar=k.par[:, g:g + 1], in1=rstd[:, b, 0:tn],
                                                 op0=ALU.mult, op1=ALU.mult).then_inc(xn_ready, 1)
                        continue
                    if i >= 2:
                        dve.wait_ge(h_ready, i - 1)
                    dve.tensor_tensor(xn[:, i % 2, 0:tn], x[:, kt, t0:t0 + tn], rstd[:, b, 0:tn],
                                      ALU.mult).then_inc(xn_ready, 1)
                    if i >= 1:
                        split_lo(dve, i - 1)
            if not final:
                split_lo(dve, len(blocks) * KT - 1)


def three(pe, out, whi, wlo, ahi, alo, start, stop):
    pe.matmul(out, whi, alo, start=start, stop=False)
    pe.matmul(out, wlo, ahi, start=False, stop=False)
    return pe.matmul(out, whi, ahi, start=False, stop=stop)


def swiglu(nc, k, tag, x, n, which, v, hi, lo, d_w):
    blocks = halves(n)
    nb = len(blocks)
    rounds = FT // 2
    PIECES, RAW = 6, 3
    units = 2 * nb
    ys = KT * nb
    with Phase(nc, tag) as ph:
        raw = ph.sb("w_raw", [P, RAW, KT, P])
        wh = ph.sb("w_hi", [P, PIECES, KT, P], F32R)
        wl = ph.sb("w_lo", [P, PIECES, KT, P], F32R)
        ah = ph.sb("a_hi", [P, 2, n], F32R)
        al = ph.sb("a_lo", [P, 2, n], F32R)
        sg = ph.sb("silu_g", [P, 2, BANK])
        aw = ph.sb("a_whole", [P, 2, BANK])
        ps = ph.psum(8)
        loaded = [ph.sem(f"w_loaded{s}") for s in range(RAW)]
        hi_done = [ph.sem(f"w_hi_done{s}") for s in range(RAW)]
        lo_done = [ph.sem(f"w_lo_done{s}") for s in range(RAW)]
        gu_ready = [ph.sem(s) for s in ("gate_ready", "up_ready")]
        y_ready, y_added = [ph.sem(s) for s in ("y_ready", "y_added")]
        sg_ready, aw_ready, ah_ready, al_ready = [
            ph.sem(s) for s in ("silu_ready", "a_ready", "a_hi_ready", "a_lo_ready")]
        block = ph.block()

        @block.sync
        def _(sp):
            with sp.Fori(0, rounds) as g:
                for j in range(PIECES):
                    sp.wait_ge(hi_done[j % RAW], 2 * g + j // RAW)
                    sp.wait_ge(lo_done[j % RAW], 2 * g + j // RAW)
                    sp.dma_start(raw[:, j % RAW], d_w[PIECES * g + j]).then_inc(loaded[j % RAW], 16)

        def split_hi(act, g, j, first=False):
            s = j % RAW
            if not first:
                act.wait_ge(*((gu_ready[j % 2], units * (g - 1) + (j // 2 + 1) * nb) if j < 4 else (y_ready, ys * g)))
            act.wait_ge(loaded[s], 16 * (2 * g + j // RAW + 1))
            act.copy(wh[:, j], raw[:, s]).then_inc(hi_done[s], 1)

        def split_lo(dve, g, j):
            s = j % RAW
            dve.wait_ge(hi_done[s], 2 * g + j // RAW + 1)
            dve.tensor_tensor(wl[:, j], raw[:, s], wh[:, j].bitcast(F32), ALU.subtract).then_inc(lo_done[s], 1)

        def ahead(u):
            return [] if u < nb else [0, 1] if nb == 1 else [u - nb]

        def act_round(act, g, last):
            for u in range(units):
                f, (t0, tn) = u // nb, blocks[u % nb]
                act.wait_ge(gu_ready[0], units * g + u + 1)
                act.activation(sg[:, u % 2, 0:tn], ps[:, 2 * (u % 2), 0:tn], ACT.Silu).then_inc(sg_ready, 1)
                if u % nb == 0:
                    split_hi(act, g, 4 + f)
                act.wait_ge(aw_ready, units * g + u + 1)
                act.copy(ah[:, f, t0:t0 + tn], aw[:, u % 2, 0:tn]).then_inc(ah_ready, 1)
                for j in () if last else ahead(u):
                    split_hi(act, g + 1, j)
            for j in () if last else (2, 3):
                split_hi(act, g + 1, j)

        @block.scalar
        def _(act):
            for j in range(4):
                split_hi(act, 0, j, first=True)
            with act.Fori(0, rounds - 1) as g:
                act_round(act, g, False)
            act_round(act, rounds - 1, True)

        def dve_round(dve, g, last):
            for u in range(units):
                f, (t0, tn) = u // nb, blocks[u % nb]
                dve.wait_ge(gu_ready[1], units * g + u + 1)
                dve.wait_ge(sg_ready, units * g + u + 1)
                dve.tensor_tensor(aw[:, u % 2, 0:tn], sg[:, u % 2, 0:tn], ps[:, 2 * (u % 2) + 1, 0:tn],
                                  ALU.mult).then_inc(aw_ready, 1)
                if u % nb == 0:
                    split_lo(dve, g, 4 + f)
                dve.wait_ge(ah_ready, units * g + u + 1)
                dve.tensor_tensor(al[:, f, t0:t0 + tn], aw[:, u % 2, 0:tn], ah[:, f, t0:t0 + tn].bitcast(F32),
                                  ALU.subtract).then_inc(al_ready, 1)
                for j in () if last else ahead(u):
                    split_lo(dve, g + 1, j)
            for y in range(ys):
                o, (t0, tn) = y % KT, blocks[y // KT]
                xs = x[:, o, t0:t0 + tn]
                dve.wait_ge(y_ready, ys * g + y + 1)
                dve.scalar_tensor_tensor(out=xs, in0=ps[:, 4 + y % 4, 0:tn], scalar=k.gate[:, which, v, o:o + 1],
                                         in1=xs, op0=ALU.mult, op1=ALU.add).then_inc(y_added, 1)
                if not last and y % (ys // 2) == 0:
                    split_lo(dve, g + 1, 2 + y // (ys // 2))

        @block.vector
        def _(dve):
            for j in range(4):
                split_lo(dve, 0, j)
            with dve.Fori(0, rounds - 1) as g:
                dve_round(dve, g, False)
            dve_round(dve, rounds - 1, True)

        @block.tensor
        def _(pe):
            with pe.Fori(0, rounds) as g:
                for u in range(units):
                    f, (t0, tn) = u // nb, blocks[u % nb]
                    for half in range(2):
                        j = 2 * f + half
                        if u % nb == 0:
                            pe.wait_ge(lo_done[j % RAW], 2 * g + j // RAW + 1)
                        pe.wait_ge(aw_ready, units * g + max(u - 1, 0))
                        for kt in range(KT):
                            mm = three(pe, ps[:, 2 * (u % 2) + half, 0:tn], wh[:, j, kt], wl[:, j, kt],
                                       hi[:, kt, t0:t0 + tn], lo[:, kt, t0:t0 + tn], kt == 0, kt == KT - 1)
                        mm.then_inc(gu_ready[half], 1)
                for f in range(2):
                    pe.wait_ge(lo_done[(4 + f) % RAW], 2 * g + (4 + f) // RAW + 1)
                for y in range(ys):
                    (b, o), (t0, tn) = divmod(y, KT), blocks[y // KT]
                    if o == 0:
                        pe.wait_ge(al_ready, units * g + nb + b + 1)
                    pe.wait_ge(y_added, ys * g + max(y - 3, 0))
                    for f in range(2):
                        mm = three(pe, ps[:, 4 + y % 4, 0:tn], wh[:, 4 + f, o], wl[:, 4 + f, o],
                                   ah[:, f, t0:t0 + tn], al[:, f, t0:t0 + tn], f == 0, f == 1)
                    mm.then_inc(y_ready, 1)


def project(nc, k, tag, n_tiles, d_w, srcs, kind, d_out=None, par0=None):
    nb = len(srcs)
    n = sum(s[2] for s in srcs)
    at = [sum(s[2] for s in srcs[:b]) for b in range(nb)]
    shift, residual = kind == "shift", kind == "residual"
    rounds = (n_tiles - 1) // 2
    tail = range(2 * rounds, n_tiles)
    with Phase(nc, tag) as ph:
        raw = ph.sb("w_raw", [P, 2, KT, P])
        wh, wl = ph.sb("w_hi", [P, 2, KT, P], F32R), ph.sb("w_lo", [P, 2, KT, P], F32R)
        if not residual:
            stage = ph.sb("stage", [P, 2, n])
        if shift:
            pad = ph.sb("padded", [P, TOK + 3])
            rest = ph.sb("mu_rest", [P, RW_TILES])
            segments = ((1, 0, CTX), (CTX + 2, CTX, SEQ))
            pad_at = (CTX + 2, CTX + 2 + BANK, 1)
        ps = ph.psum(2 * nb)
        loaded = [ph.sem(f"w_loaded{s}") for s in range(2)]
        stored = [ph.sem(f"stored{s}") for s in range(2)]
        hi_done, lo_done, out_ready, evicted, added, shift_step, pads_ready = ph.sems(
            "w_hi_done w_lo_done out_ready evicted added shift_step pads_ready")
        block = ph.block()

        def load(sp, t, s, first=False):
            if not first:
                sp.wait_ge(lo_done, t - 1)
            sp.dma_start(raw[:, s], d_w[t]).then_inc(loaded[s], 16)

        def store(sp, t, s):
            if residual:
                return
            if shift:
                sp.wait_ge(shift_step, 6 * (t + 1) + 1)
                sp.dma_start(d_out[t][:, TOK:], stage[:, s, 0:CTX]).then_inc(stored[s], 16)
            else:
                sp.wait_ge(evicted, nb * (t + 1))
            sp.dma_start(d_out[t][:, 0:n], stage[:, s, :]).then_inc(stored[s], 16)

        def stores_before(i):
            return i * (32 if shift else 16)

        @block.sync
        def _(sp):
            load(sp, 0, 0, first=True)
            with sp.Fori(0, rounds) as i:
                load(sp, 2 * i + 1, 1)
                load(sp, 2 * i + 2, 0)
                store(sp, 2 * i, 0)
                store(sp, 2 * i + 1, 1)
            if n_tiles % 2 == 0:
                load(sp, n_tiles - 1, 1)
            for t in tail:
                store(sp, t, t % 2)
            if not residual:
                for s in range(2):
                    sp.wait_ge(stored[s], stores_before(len(range(s, n_tiles, 2))))

        def split_hi(act, t, s, i, first=False):
            if not first:
                act.wait_ge(out_ready, nb * (t - 1))
            act.wait_ge(loaded[s], 16 * (i + 1))
            act.copy(wh[:, s], raw[:, s]).then_inc(hi_done, 1)

        def evict(act, t, s, i):
            if residual:
                return
            if shift:
                act.wait_ge(shift_step, 6 * t + 1)
            else:
                act.wait_ge(stored[s], stores_before(i))
            for b, (_, _, tn) in enumerate(srcs):
                src = ps[:, s * nb + b, 0:tn]
                wait_apart(act, hi_done, out_ready, nb * t + b + 1)
                if shift:
                    act.copy(pad[:, pad_at[b]:pad_at[b] + tn], src).then_inc(evicted, 1)
                elif kind == "gate":
                    act.activation(stage[:, s, at[b]:at[b] + tn], src, ACT.Sigmoid,
                                   bias=k.par[:, bass.ds(t + par0, 1)]).then_inc(evicted, 1)
                else:
                    act.mul(stage[:, s, at[b]:at[b] + tn], src, par0).then_inc(evicted, 1)

        @block.scalar
        def _(act):
            split_hi(act, 0, 0, 0, first=True)
            if shift:
                act.wait_ge(pads_ready, 3)
            with act.Fori(0, rounds) as i:
                split_hi(act, 2 * i + 1, 1, i)
                evict(act, 2 * i, 0, i)
                split_hi(act, 2 * i + 2, 0, i + 1)
                evict(act, 2 * i + 1, 1, i)
            for t in tail:
                if t + 1 < n_tiles:
                    split_hi(act, t + 1, (t + 1) % 2, (t + 1) // 2)
                evict(act, t, t % 2, t // 2)

        def split_lo(dve, t, s):
            dve.wait_ge(hi_done, t + 1)
            dve.tensor_tensor(wl[:, s], raw[:, s], wh[:, s].bitcast(F32), ALU.subtract).then_inc(lo_done, 1)

        def finish(dve, t, s, i):
            if residual:
                for b, (_, _, tn) in enumerate(srcs):
                    xs = k.x[:, bass.ds(t, 1), at[b]:at[b] + tn].squeeze(1)
                    dve.wait_ge(out_ready, nb * t + b + 1)
                    dve.scalar_tensor_tensor(out=xs, in0=ps[:, s * nb + b, 0:tn], scalar=k.gate[:, 1, 0, bass.ds(t, 1)],
                                             in1=xs, op0=ALU.mult, op1=ALU.add).then_inc(added, 1)
            if shift:
                mp, mn = PAR["mu_prev"][0], PAR["mu_next"][0]
                dve.wait_ge(evicted, nb * (t + 1))
                dve.wait_ge(stored[s], stores_before(i))
                for a, o, m in segments:
                    dve.tensor_scalar(stage[:, s, o:o + m], pad[:, a:a + m], rest[:, bass.ds(t, 1)], None,
                                      ALU.mult).then_inc(shift_step, 1)
                for step, (mu, d) in enumerate(((mp, -1), (mn, 1))):
                    for q, (a, o, m) in enumerate(segments):
                        dve.wait_ge(shift_step, 6 * t + 2 * step + q + 2)
                        dve.scalar_tensor_tensor(out=stage[:, s, o:o + m], in0=pad[:, a + d:a + d + m],
                                                 scalar=k.par[:, bass.ds(t + mu, 1)], in1=stage[:, s, o:o + m],
                                                 op0=ALU.mult, op1=ALU.add).then_inc(shift_step, 1)

        @block.vector
        def _(dve):
            if shift:
                mp, mn = PAR["mu_prev"][0], PAR["mu_next"][0]
                for z in (0, CTX + 1, TOK + 2):
                    dve.memset(pad[:, z:z + 1], 0.0).then_inc(pads_ready, 1)
                dve.tensor_tensor(rest[:], k.par[:, mp:mp + RW_TILES], k.par[:, mn:mn + RW_TILES],
                                  ALU.add).then_inc(pads_ready, 1)
                dve.wait_ge(pads_ready, 4)
                dve.tensor_scalar(rest[:], rest[:], -1.0, 1.0, ALU.mult, ALU.add).then_inc(shift_step, 1)
                dve.wait_ge(shift_step, 1)
            split_lo(dve, 0, 0)
            with dve.Fori(0, rounds) as i:
                split_lo(dve, 2 * i + 1, 1)
                finish(dve, 2 * i, 0, i)
                split_lo(dve, 2 * i + 2, 0)
                finish(dve, 2 * i + 1, 1, i)
            for t in tail:
                if t + 1 < n_tiles:
                    split_lo(dve, t + 1, (t + 1) % 2)
                finish(dve, t, t % 2, t // 2)

        def product(pe, t, s, i):
            pe.wait_ge(lo_done, t + 1)
            pe.wait_ge(added if residual else evicted, nb * 2 * i)
            if s:
                pe.wait_ge(added if residual else evicted, nb * (2 * i + s - 1))
            for b, (h_hi, h_lo, tn) in enumerate(srcs):
                for kt in range(KT):
                    mm = three(pe, ps[:, s * nb + b, 0:tn], wh[:, s, kt], wl[:, s, kt], h_hi[:, kt], h_lo[:, kt],
                               kt == 0, kt == KT - 1)
                mm.then_inc(out_ready, 1)

        @block.tensor
        def _(pe):
            with pe.Fori(0, rounds) as i:
                for s in range(2):
                    product(pe, 2 * i + s, s, i)
            for t in tail:
                product(pe, t, t % 2, t // 2)


def project_v(nc, k, hi, lo, hi_c, lo_c, d_w, d_out):
    n_tiles = TOK // P
    NV = HEADS * HD
    with Phase(nc, "pv") as ph:
        raw = ph.sb("w_raw", [P, KT, NV])
        wh, wl = ph.sb("w_hi", [P, KT, NV], F32R), ph.sb("w_lo", [P, KT, NV], F32R)
        stage = ph.sb("stage", [P, 2, NV])
        ps = ph.psum(4)
        loaded, hi_done, lo_done, out_ready, evicted = ph.sems("w_loaded w_hi_done w_lo_done out_ready evicted")
        stored = [ph.sem(f"stored{s}") for s in range(2)]
        x_kept = ph.sem("x_kept")
        block = ph.block()
        QUARTERS = [range(q, q + 2) for q in range(0, KT, 2)]

        @block.sync
        def _(sp):
            for q in QUARTERS:
                sp.dma_start(raw[:, q[0]:q[-1] + 1], d_w[:, q[0]:q[-1] + 1]).then_inc(loaded, 16)
                sp.wait_ge(loaded, 16 * (q[0] // 2 + 1))
            sp.dma_start(k.d_x_kept, k.x[:]).then_inc(x_kept, 16)
            for t in range(n_tiles):
                sp.wait_ge(evicted, t + 1)
                sp.dma_start(d_out[t], stage[:, t % 2]).then_inc(stored[t % 2], 16)
            for s in range(2):
                sp.wait_ge(stored[s], 16 * (n_tiles // 2))
            sp.wait_ge(x_kept, 16)

        @block.scalar
        def _(act):
            for i, q in enumerate(QUARTERS):
                act.wait_ge(loaded, 16 * (i + 1))
                act.copy(wh[:, q[0]:q[-1] + 1], raw[:, q[0]:q[-1] + 1]).then_inc(hi_done, 1)
            for t in range(n_tiles):
                act.wait_ge(out_ready, t + 1)
                if t >= 2:
                    act.wait_ge(stored[t % 2], 16 * (t // 2))
                act.copy(stage[:, t % 2], ps[:, t % 4]).then_inc(evicted, 1)

        @block.vector
        def _(dve):
            for i, q in enumerate(QUARTERS):
                a, b = q[0], q[-1] + 1
                dve.wait_ge(hi_done, i + 1)
                dve.tensor_tensor(wl[:, a:b], raw[:, a:b], wh[:, a:b].bitcast(F32), ALU.subtract).then_inc(lo_done, 1)

        @block.tensor
        def _(pe):
            for t in range(n_tiles):
                h, l, a = (hi, lo, t * P) if t < SEQ // P else (hi_c, lo_c, t * P - SEQ)
                if t >= 4:
                    pe.wait_ge(evicted, t - 3)
                for kt in range(KT):
                    if t == 0 and kt % 2 == 0:
                        pe.wait_ge(lo_done, kt // 2 + 1)
                    mm = three(pe, ps[:, t % 4], h[:, kt, a:a + P], l[:, kt, a:a + P], wh[:, kt], wl[:, kt],
                               kt == 0, kt == KT - 1)
                mm.then_inc(out_ready, 1)


def attention(nc, k, d_q, d_k, d_v, d_rpb):
    PAIRS = ROWS // 2
    E = 2 * WIN_H
    LOC = (WIN_H + 1) * GRID_W
    TILES = TOK // P

    def window(p):
        i = 2 * p
        r0, r1 = (min(max(r - WIN_H // 2, 0), ROWS - WIN_H) for r in (i, i + 1))
        return r0, r1 - r0 + WIN_H, r0 - i + WIN_H - 1

    with Phase(nc, "na") as ph:
        q, kk, vv = ph.sb("q", [P, HP, SEQ]), ph.sb("k", [P, HP, TOK]), ph.sb("v", [P, TILES, HEADS * HD])
        qz = ph.sb("q_of_head", [P, 2, SEQ])
        rpb = ph.sb("rpb", [P, HP, 2, E, GRID_W])
        edge = ph.sb("bias_edge", [P, 2, E, GRID_W])
        inner = ph.sb("bias_inner", [P, 2, WIN_H + 1, GRID_W])
        outside = ph.sb("outside", [P, WIN_H + 1, GRID_W])
        sb_ = ph.sb("s_biased", [P, 2, LOC])
        pr = ph.sb("probs", [P, 2, LOC + CTX])
        prT = ph.sb("probs_t", [P, 2, 7, P])
        o = ph.sb("o", [P, 2, P])
        stat = ph.sb("stat", [P, 2, 8])
        ps = ph.psum(8)
        S_BANK, T_BANK, O_BANK, OT_BANK = (0, 2), 4, 6, 7
        (in_loaded, rpb_loaded, bias_built, mask_step, qz_ready, s_ready, m_step, neg_ready, e_ready,
         t_ready, pt_dve, pt_act, o_ready, o_scaled, den_step, ot_ready, ot_done, zeroed, mask_copied) = ph.sems(
            "in_loaded rpb_loaded bias_built mask_step qz_ready s_ready m_step neg_ready e_ready t_ready "
            "pt_dve pt_act o_ready o_scaled den_step ot_ready ot_done zeroed mask_copied")
        x_back = ph.sem("x_back")
        block = ph.block()
        U = 2 * PAIRS
        units = [(p, s) for p in range(PAIRS) for s in range(2)]

        @block.sync
        def _(sp):
            for hp in range(HP):
                sp.dma_start(q[:, hp], d_q[hp]).then_inc(in_loaded, 16)
                sp.dma_start(kk[:, hp], d_k[hp]).then_inc(in_loaded, 16)
            sp.dma_start(vv[:], d_v.rearrange("t p c -> p t c")).then_inc(in_loaded, 16)
            for h in range(HEADS):
                for row in range(2):
                    sp.dma_start(rpb[row * GRID_W:(row + 1) * GRID_W, h // 2, h % 2],
                                 d_rpb[h][:, 1 - row:1 - row + E]).then_inc(rpb_loaded, 16)
            sp.dma_start(k.x[:], k.d_x_kept).then_inc(x_back, 16)
            sp.wait_ge(rpb_loaded, 32 * HEADS)
            sp.wait_ge(x_back, 16)

        @block.gpsimd
        def _(pool):
            first, lim, back = outside[0:GRID_W], GRID_W - WIN_W, WIN_W // 2
            pool.memset(outside[:], 0.0).then_inc(mask_step, 1)
            pool.wait_ge(mask_step, 1)
            pool.affine_select(out=first[:, :, 0:lim], in_=first[:, :, 0:lim], compare_op=ALU.is_ge, fill=MASKED,
                               base=back, pattern=[[0, WIN_H + 1], [1, lim]],
                               channel_multiplier=-1).then_inc(mask_step, 1)
            pool.wait_ge(mask_step, 2)
            pool.affine_select(out=first[:, :, WIN_W:], in_=first[:, :, WIN_W:], compare_op=ALU.is_ge, fill=MASKED,
                               base=-back - 1, pattern=[[0, WIN_H + 1], [-1, lim]],
                               channel_multiplier=1).then_inc(mask_step, 1)
            pool.wait_ge(mask_step, 3)
            pool.dma_start(outside[GRID_W:P], first).then_inc(mask_copied, 16)
            pool.wait_ge(mask_copied, 16)
            pool.memset(outside[0:GRID_W, WIN_H], MASKED).then_inc(mask_step, 1)
            pool.memset(outside[GRID_W:P, 0], MASKED).then_inc(mask_step, 1)

        MASK_STEPS = 5

        @block.scalar
        def _(act):
            act.wait_ge(in_loaded, 16 * (2 * HP + 1))
            act.wait_ge(zeroed, 2)
            with act.Fori(0, HP) as hp:
                for s in range(2):
                    a, b = s * HD, (s + 1) * HD
                    act.wait_ge(s_ready, U * hp)
                    act.copy(qz[a:b, s, :], q[a:b, bass.ds(hp, 1), :].squeeze(1)).then_inc(qz_ready, 1)

                def exps(u):
                    p, s = units[u]
                    L = window(p)[1] * GRID_W
                    act.wait_ge(neg_ready, U * hp + u + 1)
                    if u >= 2:
                        act.wait_ge(t_ready, U * hp + u - 1)
                    else:
                        act.wait_ge(t_ready, U * hp)
                    act.activation(pr[:, s, 0:L], sb_[:, s, 0:L], ACT.Exp, bias=stat[:, s, 2:3],
                                   accum_out=stat[:, s, 3:4])
                    act.activation(pr[:, s, L:L + CTX], ps[:, S_BANK[s] + 1, BANK - CTX:BANK], ACT.Exp,
                                   bias=stat[:, s, 2:3], accum_out=stat[:, s, 4:5]).then_inc(e_ready, 1)

                def probs_t(u):
                    act.wait_ge(t_ready, U * hp + u + 1)
                    act.copy(prT[:, units[u][1], 4:7], ps[:, T_BANK + 1, 0:3 * P].rearrange("p (t q) -> p t q", q=P)).then_inc(pt_act, 1)

                for u in range(U + 1):
                    if u < U:
                        exps(u)
                    if u >= 1:
                        probs_t(u - 1)

        @block.vector
        def _(dve):
            for s in range(2):
                dve.memset(qz[(1 - s) * HD:(2 - s) * HD, s, :], 0.0).then_inc(zeroed, 1)
            dve.memset(ps[:, T_BANK + 1, 0:3 * P], 0.0).then_inc(zeroed, 1)
            dve.wait_ge(mask_step, MASK_STEPS)
            dve.wait_ge(rpb_loaded, 32 * HEADS)
            with dve.Fori(0, HP) as hp:
                raw_bias = rpb[:, bass.ds(hp, 1)].squeeze(1)
                for s in range(2):
                    dve.tensor_tensor(edge[:, s], raw_bias[:, s], outside[:, 1:2, :].to_broadcast([P, E, GRID_W]),
                                      ALU.add).then_inc(bias_built, 1)
                    dve.tensor_tensor(inner[:, s], raw_bias[:, s, WIN_H // 2 - 1:WIN_H // 2 + WIN_H], outside[:],
                                      ALU.add).then_inc(bias_built, 1)
                dve.wait_ge(bias_built, 4 * (hp + 1))

                def biased(u):
                    p, s = units[u]
                    r0, rows, e0 = window(p)
                    L = rows * GRID_W
                    table = edge[:, s, e0:e0 + rows] if rows == WIN_H else inner[:, s]
                    dve.wait_ge(s_ready, U * hp + u + 1)
                    S = ps[:, S_BANK[s]:S_BANK[s] + 2].rearrange("p b c -> p (b c)")
                    dve.tensor_reduce(stat[:, s, 0:1], S[:, 2 * BANK - CTX:], AX.X, ALU.max).then_inc(m_step, 1)
                    wait_apart(dve, bias_built, e_ready, U * hp + max(u - 1, 0))
                    dve.tensor_tensor_reduce(out=sb_[:, s, 0:L], in0=S[:, 0:L], in1=table.rearrange("p r c -> p (r c)"),
                                             scale=1.0, scalar=MASKED, op0=ALU.add, op1=ALU.max,
                                             accum_out=stat[:, s, 1:2]).then_inc(m_step, 1)
                    dve.wait_ge(m_step, 2 * (U * hp + u + 1))
                    dve.tensor_scalar(stat[:, s, 2:3], stat[:, s, 1:2], stat[:, s, 0:1], -1.0, ALU.max,
                                      ALU.mult).then_inc(neg_ready, 1)

                def probs_t(u):
                    dve.wait_ge(t_ready, U * hp + u + 1)
                    dve.tensor_copy(prT[:, units[u][1], 0:4], ps[:, T_BANK].rearrange("p (t q) -> p t q", q=P)).then_inc(pt_dve, 1)
                    s = units[u][1]
                    dve.wait_ge(e_ready, U * hp + u + 1)
                    dve.tensor_tensor(stat[:, s, 5:6], stat[:, s, 3:4], stat[:, s, 4:5], ALU.add).then_inc(den_step, 1)
                    dve.wait_ge(den_step, 2 * (U * hp + u) + 1)
                    dve.reciprocal(stat[:, s, 6:7], stat[:, s, 5:6]).then_inc(den_step, 1)

                def scaled(u):
                    p, s = units[u]
                    dve.wait_ge(o_ready, U * hp + u + 1)
                    dve.wait_ge(den_step, 2 * (U * hp + u + 1))
                    if p >= 2:
                        dve.wait_ge(ot_ready, PAIRS * hp + p - 1)
                    else:
                        dve.wait_ge(ot_ready, PAIRS * hp)
                    dve.tensor_scalar(o[:, p % 2, s * HD:(s + 1) * HD], ps[:, O_BANK, 0:HD], stat[:, s, 6:7], None,
                                      ALU.mult).then_inc(o_scaled, 1)

                def out(p):
                    dve.wait_ge(ot_ready, PAIRS * hp + p + 1)
                    dve.tensor_copy(k.o_na[:, bass.ds(hp, 1), p * P:(p + 1) * P].squeeze(1),
                                    ps[:, OT_BANK, 0:P]).then_inc(ot_done, 1)

                for u in range(U + 3):
                    if u < U:
                        biased(u)
                    if 1 <= u <= U:
                        probs_t(u - 1)
                    if 2 <= u < U + 2:
                        scaled(u - 2)
                    if u >= 4 and u % 2 == 0:
                        out((u - 4) // 2)

        @block.tensor
        def _(pe):
            pe.wait_ge(in_loaded, 16 * (2 * HP + 1))
            pe.wait_ge(zeroed, 3)
            with pe.Fori(0, HP) as hp:
                def scores(u):
                    p, s = units[u]
                    r0, rows, _ = window(p)
                    if u < 2:
                        pe.wait_ge(qz_ready, 2 * hp + s + 1)
                        pe.wait_ge(e_ready, U * hp)
                    else:
                        pe.wait_ge(e_ready, U * hp + u - 1)
                    lhs = qz[:, s, p * P:(p + 1) * P]
                    keys = kk[:, bass.ds(hp, 1), :].squeeze(1)
                    a = r0 * GRID_W
                    pe.matmul(ps[:, S_BANK[s]], lhs, keys[:, a:a + BANK], start=True, stop=True)
                    if rows > WIN_H:
                        pe.matmul(ps[:, S_BANK[s] + 1, 0:GRID_W], lhs, keys[:, a + BANK:a + BANK + GRID_W],
                                  start=True, stop=True)
                    pe.matmul(ps[:, S_BANK[s] + 1, BANK - CTX:BANK], lhs, keys[:, SEQ:TOK], start=True,
                              stop=True).then_inc(s_ready, 1)

                def blocks(u):
                    r0, rows, _ = window(units[u][0])
                    L = rows * GRID_W
                    loc = [(c, min(P, L - c), r0 // 2 + c // P) for c in range(0, L, P)]
                    return loc + [(L + c, P, (SEQ + c) // P) for c in range(0, CTX, P)]

                def transposes(u):
                    s = units[u][1]
                    pe.wait_ge(e_ready, U * hp + u + 1)
                    pe.wait_ge(pt_dve, U * hp + u)
                    pe.wait_ge(pt_act, U * hp + u)
                    for j, (c, m, _) in enumerate(blocks(u)):
                        mm = pe.transpose(ps[0:m, T_BANK + j // 4, (j % 4) * P:(j % 4 + 1) * P], pr[:, s, c:c + m],
                                          k.ident[:])
                    mm.then_inc(t_ready, 1)

                def values(u):
                    s = units[u][1]
                    pe.wait_ge(pt_dve, U * hp + u + 1)
                    pe.wait_ge(pt_act, U * hp + u + 1)
                    pe.wait_ge(o_scaled, U * hp + u)
                    bl = blocks(u)
                    for j, (_, m, t) in enumerate(bl):
                        mm = pe.matmul(ps[:, O_BANK, 0:HD], prT[0:m, s, j], vv[0:m, t, bass.ds(hp * P + s * HD, HD)],
                                       start=j == 0, stop=j == len(bl) - 1)
                    mm.then_inc(o_ready, 1)

                def out(p):
                    pe.wait_ge(o_scaled, U * hp + 2 * p + 2)
                    pe.wait_ge(ot_done, PAIRS * hp + p)
                    pe.transpose(ps[:, OT_BANK, 0:P], o[:, p % 2], k.ident[:]).then_inc(ot_ready, 1)

                for u in range(U + 3):
                    if u < U:
                        scores(u)
                    if 1 <= u <= U:
                        transposes(u - 1)
                    if 2 <= u < U + 2:
                        values(u - 2)
                    if u >= 4 and u % 2 == 0:
                        out((u - 4) // 2)


LEVELS = 7


def rwkv_masks(pool, k, same, work, step, same_ready, masks_ready):
    steps = Chain(pool, step)

    def select(out, in_, base, pattern, mult):
        steps.done(pool.affine_select(out=out, in_=in_, compare_op=ALU.is_ge, fill=0.0, base=base, pattern=pattern,
                                      channel_multiplier=mult))
        steps.wait()

    def blocks_of(out, size):
        v = out.rearrange("p (b c) -> p b c", c=size)
        steps.done(pool.memset(out, 1.0))
        steps.wait()
        select(v, v, 0, [[-size, P // size], [0, size]], 1)
        select(v, v, size - 1, [[size, P // size], [0, size]], -1)

    by_head = HD.bit_length() - 1
    blocks_of(same[:, by_head], HD)
    pool.tensor_copy(k.same64[:], same[:, by_head]).then_inc(same_ready, 1)
    for l in range(LEVELS + 1):
        if l != by_head:
            blocks_of(same[:, l], 1 << l)
    lower, upper = (1, [[-1, P]]), (-1, [[1, P]])
    ring = [work[:, w % work.shape[1]] for w in range(2 * (LEVELS + 2))]
    for d in range(2):
        mult, pattern = (upper, lower)[d]
        for inclusive in range(2):
            t = ring.pop()
            select(t, same[:, LEVELS], inclusive - 1, pattern, mult)
            for h in range(2):
                steps.done(pool.tensor_copy(k.keep[:, d, h, inclusive], t))
        mult, pattern = (lower, upper)[d]
        for l in range(LEVELS):
            t = ring.pop()
            steps.done(pool.tensor_tensor(t, same[:, l + 1], same[:, l], ALU.subtract))
            steps.wait()
            select(t, t, 0, pattern, mult)
            steps.done(pool.tensor_tensor(k.level[:, d, l], t, k.ident[:], ALU.add))
    steps.wait()
    pool.memset(work[:, 0], 0.0).then_inc(masks_ready, 1)


def rwkv(nc, k, d_rw, d_wup, d_aup, d_gup):
    L = NCH * CH
    OFF = (0, CTX)
    MID = (CH // 2 - 1, CH // 2)
    END = (CH - 1, 0)
    SC = STREAM // CH
    ROUNDS = NCH // 2
    CHAINS = [(s, d) for s in range(2) for d in range(2)]
    BLOCKS, SBLOCKS = halves(L), halves(STREAM)
    NZ = 4 * len(BLOCKS)
    DVE_PER_PAIR = 42
    with Phase(nc, "rw") as ph:
        tw, al = ph.sb("tanh_w", [P, STREAM]), ph.sb("a_in", [P, STREAM])
        sgl = ph.sb("sigmoid_g", [P, SEQ])
        r, kf, v = ph.sb("r", [P, STREAM]), ph.sb("k", [P, STREAM]), ph.sb("v", [P, STREAM])
        kk = ph.sb("kk", [P, STREAM])
        ytok = kk[:].rearrange("p (c f) -> p c f", f=CH)
        vtok = ph.sb("v_tok", [P, SC, CH])
        ar = ph.sb("alpha_rho", [P, 2, 2, L])
        bk = ph.sb("beta_kappa", [P, 2, 2, L])
        e = ph.sb("e", [P, L])
        small = ph.sb("decays", [P, 2, 4, NCH])
        lw, la = ph.sb("w_up", [P, 2, P]), ph.sb("a_up", [P, 2, P])
        gup = ph.sb("g_up", [P, P])
        rest = ph.sb("rest", [P, HP])
        stat = ph.sb("gn_stat", [P, 4, 2 * SEQ // P])
        def over(buf):
            return buf[:, 0:4 * 2 * CH].rearrange("p (s d i t) -> p s d i t", s=2, d=2, i=2)
        bk_s, bke, it = over(kf), over(r), over(e)
        ar_s, arz = ph.sb("ar_s", [P, 2, 2, 2, CH]), ph.sb("ar_of_head", [P, 2, 2, 2, 2, CH])
        bket = ph.sb("bk_end_tok", [P, 2, 2, 2, CH])
        ab, kr = ph.sb("ab", [P, 2, 2, 2, 2, CH]), ph.sb("kr", [P, 2, 2, 2, 2, CH])
        atr = ph.sb("a_t", [P, 2, 2, 2, CH], F32R)
        inv = ph.sb("inverse", [P, 2, 2, 2, 2, CH], F32R)
        tb, ttb = inv[:, :, :, 0], inv[:, :, :, 1]
        pl = ph.sb("joined", [P, 2, 2, 2, 2, CH], F32R)
        er = ph.sb("residual", [P, 2, 2, 2, CH], F32R)
        ttf = ph.sb("t_newton_t", [P, 2, 2, 2, CH])
        wsb, usb = ph.sb("w", [P, 2, CH]), ph.sb("u", [P, 2, CH])
        sbd = ph.sb("state", [P, 2, 2, P])
        ps = ph.psum(8)

        def bank(s, d, i):
            return ps[:, 4 * s + 2 * d + i]

        def half(s, d, q):
            return bank(s, d, q // 2)[:, (q % 2) * 2 * CH:(q % 2 + 1) * 2 * CH]

        T_HALF, TT_HALF, S_HALF, P_HALF = range(4)

        def inverses(s, d, l):
            first = 0 if l else 1
            return (inv[:, s, d, first:].rearrange("p k h t -> p (k h t)"), bank(s, d, 0)[:, first * 2 * CH:])

        def flat(a):
            return a.rearrange("p h t -> p (h t)")

        (lora_loaded, hp_loaded, lora_ready, zeroed, go, sq_ready, kk_sum, kk_inv, kk_rstd, za_ready, za_evicted,
         bonus_in, bonus_ps, log_ready, e_ready, ar_ready, vt_ready, vt_copied, bulk_ready, centred, gn_sq, gn_inv,
         gn_rstd, normed, ln_ps, ln_done, gate_ps, pair_done, dve_step) = ph.sems(
            "lora_loaded hp_loaded lora_ready zeroed go sq_ready kk_sum kk_inv kk_rstd za_ready za_evicted "
            "bonus_in bonus_ps log_ready e_ready ar_ready vt_ready vt_copied bulk_ready centred gn_sq gn_inv "
            "gn_rstd normed ln_ps ln_done gate_ps pair_done dve_step")

        def per_dir(names):
            return [[ph.sem(f"{name}{d}") for d in range(2)] for name in names.split()]

        def per_chain(names):
            return [[[ph.sem(f"{name}{s}{d}") for d in range(2)] for s in range(2)] for name in names.split()]

        (staged, arz_ready, m_ready, masked, at_ready, bke_ready, tr_ready, tr_copied, p_ready, pl_ready, t_ready,
         t_copied, g_ready, it_ready, er_ready, n_ready, ttf_ready, y_ready) = per_chain(
            "staged arz_ready m_ready masked at_ready bke_ready tr_ready tr_copied p_ready pl_ready t_ready t_copied "
            "g_ready it_ready er_ready n_ready ttf_ready y_ready")
        w_ready, w_copied, u_ready, u_copied, st_ready, st_done, y_added = per_dir(
            "w_ready w_copied u_ready u_copied st_ready st_done y_added")
        mask_step, same_ready, masks_ready, tables_copied = ph.sems("mask_step same_ready masks_ready tables_copied")
        block = ph.block()

        def par(name, i):
            return k.par[:, bass.ds(i + PAR[name][0], 1)]

        def place(d, n, last=NCH):
            return n if d == 0 else last - 1 - n

        def out(hp, b):
            return k.o_rw[:, bass.ds(hp, 1), b * BANK:(b + 1) * BANK].squeeze(1)

        @block.sync
        def _(sp):
            sp.dma_start(tw[:], d_rw[12]).then_inc(lora_loaded, 16)
            sp.dma_start(al[:], d_rw[13]).then_inc(lora_loaded, 16)
            sp.dma_start(sgl[:], d_rw[14][:, CTX:TOK]).then_inc(lora_loaded, 16)
            sp.wait_ge(lora_loaded, 48)
            sp.dma_start(k.d_rpb_copies, k.d_rpb_source).then_inc(tables_copied, 16)
            sp.wait_ge(zeroed, 2)
            with sp.Fori(0, HP) as hp:
                wait_apart(sp, lora_loaded, hp_loaded, 128 * hp)
                sp.wait_ge(pair_done, hp)
                for n, buf in enumerate((r, kf, v)):
                    sp.dma_start(buf[:], d_rw[hp + HP * n]).then_inc(hp_loaded, 16)
                for d in range(2):
                    for dst, src in ((lw, d_wup), (la, d_aup)):
                        sp.dma_start(dst[d * HD:(d + 1) * HD, d], src[d, :, bass.ds(hp * P, P)]).then_inc(hp_loaded, 16)
                sp.dma_start(gup[:], d_gup[:, bass.ds(hp * P, P)]).then_inc(hp_loaded, 16)
            sp.wait_ge(hp_loaded, 128 * HP)
            sp.wait_ge(tables_copied, 16)

        @block.gpsimd
        def _(pool):
            for t in (lw, la, arz, ab, kr, small):
                pool.memset(t[:], 0.0).then_inc(zeroed, 1)
            tiles = "p s d i t -> p (s d i) t"
            rwkv_masks(pool, k, bket[:].rearrange(tiles), ttf[:].rearrange(tiles), mask_step, same_ready, masks_ready)
            with pool.Fori(0, HP) as hp:
                with pool.Fori(0, ROUNDS) as i:
                    done = ROUNDS * hp + i
                    pool.wait_ge(bulk_ready, hp + 1)
                    for s, d in CHAINS:
                        c = place(d, 2 * i + s) * CH
                        wait_apart(pool, go, m_ready[s][d], 2 * done)
                        wait_apart(pool, go, bke_ready[s][d], done)
                        pool.tensor_copy(bk_s[:, s, d], bk[:, d, :, bass.ds(c, CH)]).then_inc(staged[s][d], 1)
                    for s, d in CHAINS:
                        c = place(d, 2 * i + s) * CH
                        wait_apart(pool, go, y_ready[s][d], done)
                        pool.tensor_copy(ar_s[:, s, d], ar[:, d, :, bass.ds(c, CH)]).then_inc(staged[s][d], 1)

        @block.scalar
        def _(act):
            act.wait_ge(lora_loaded, 48)
            act.activation(tw[:], tw[:], ACT.Tanh).then_inc(lora_ready, 1)
            act.activation(sgl[:], sgl[:], ACT.Sigmoid).then_inc(lora_ready, 1)
            with act.Fori(0, HP) as hp:
                wait_apart(act, go, hp_loaded, 128 * (hp + 1))
                for t0, tn in SBLOCKS:
                    act.activation(kk[:, t0:t0 + tn], kf[:, t0:t0 + tn], ACT.Square,
                                   scale=par("k_k", hp)).then_inc(sq_ready, 1)
                for i in range(NZ):
                    (d, b), q = divmod(i // 2, len(BLOCKS)), i % 2
                    t0, tn = BLOCKS[b]
                    wait_apart(act, go, za_ready, NZ * hp + i + 1)
                    act.activation((ar, bk)[q][:, d, 0, t0:t0 + tn], ps[:, 3 + i % 5, 0:tn], ACT.Sigmoid,
                                   bias=par(("w0", "a0")[q], hp + HP * d)).then_inc(za_evicted, 1)
                for b, (t0, tn) in enumerate(SBLOCKS):
                    act.wait_ge(kk_inv, len(SBLOCKS) * hp + b + 1)
                    act.activation(kk[:, t0:t0 + tn], kk[:, t0:t0 + tn], ACT.Sqrt).then_inc(kk_rstd, 1)
                for b in range(3):
                    act.wait_ge(vt_ready, 3 * hp + b + 1)
                    act.copy(vtok[:, 4 * b:4 * b + 4], ps[:, 5 + b].rearrange("p (c f) -> p c f", f=CH)).then_inc(vt_copied, 1)
                for d in range(2):
                    act.wait_ge(log_ready, 4 * hp + 2 * (d + 1))
                    act.activation(e[:], ar[:, d, 1], ACT.Exp, scale=KAPPA).then_inc(e_ready, 1)
                    act.activation(ar[:, d, 0], ar[:, d, 0], ACT.Exp, scale=-KAPPA)
                    act.activation(small[:, d, 3], small[:, d, 2], ACT.Exp, scale=-KAPPA)
                    act.activation(ar[:, d, 1], ar[:, d, 1], ACT.Exp, scale=-KAPPA).then_inc(ar_ready, 1)
                def of_head(i):
                    for s, d in CHAINS:
                        c = place(d, 2 * i + s) * CH
                        wait_apart(act, lora_ready, m_ready[s][d], 2 * (ROUNDS * hp + i))
                        for h in range(2):
                            rows = slice(h * HD, (h + 1) * HD)
                            act.copy(arz[rows, s, d, h], ar[rows, d, :, bass.ds(c, CH)]).then_inc(arz_ready[s][d], 1)

                def act_round(i, last):
                    done = ROUNDS * hp + i
                    for s, d in CHAINS:
                        act.wait_ge(tr_ready[s][d], done + 1)
                        act.copy(flat(bket[:, s, d]), half(s, d, S_HALF)).then_inc(tr_copied[s][d], 1)
                    for l in range(LEVELS):
                        for s, d in CHAINS[1:]:
                            act.wait_ge(t_ready[s][d], LEVELS * done + l + 1)
                            act.copy(*inverses(s, d, l)).then_inc(t_copied[s][d], 1)
                    if not last:
                        of_head(i + 1)
                    for s in range(2):
                        step = NCH * hp + 2 * i + s
                        for d in range(2):
                            act.wait_ge(w_ready[d], step + 1)
                            act.copy(wsb[:, d], half(s, d, S_HALF)[:, 0:CH]).then_inc(w_copied[d], 1)
                        for d in range(2):
                            act.wait_ge(u_ready[d], step + 1)
                            act.copy(usb[:, d], half(s, d, T_HALF)[:, 0:CH]).then_inc(u_copied[d], 1)

                act.wait_ge(bulk_ready, hp + 1)
                of_head(0)
                with act.Fori(0, ROUNDS - 1) as i:
                    act_round(i, False)
                act_round(ROUNDS - 1, True)
                act.wait_ge(centred, hp + 1)
                act.activation(e[:, 0:SEQ], kk[:, CTX:TOK], ACT.Square).then_inc(gn_sq, 1)
                act.wait_ge(gn_inv, hp + 1)
                act.activation(stat[:, 3], stat[:, 2], ACT.Sqrt).then_inc(gn_rstd, 1)
                for b in range(2):
                    wait_apart(act, go, ln_ps, 2 * hp + b + 1)
                    act.activation(e[:, b * BANK:(b + 1) * BANK], ps[:, b], ACT.Identity, bias=par("ln_b", hp),
                                   scale=par("ln_w", hp)).then_inc(ln_done, 1)

        @block.vector
        def _(dve):
            ka0 = PAR["k_a"][0]
            dve.tensor_scalar(rest[:], k.par[:, ka0:ka0 + HP], -1.0, 1.0, ALU.mult, ALU.add).then_inc(go, 1)
            dve.wait_ge(go, 1)
            dve.wait_ge(zeroed, 6)
            dve.wait_ge(same_ready, 1)
            dve.wait_ge(lora_ready, 2)
            with dve.Fori(0, HP) as hp:
                c = Chain(dve, dve_step, DVE_PER_PAIR * hp)
                done, wait = c.done, c.wait
                dve.wait_ge(hp_loaded, 128 * (hp + 1))
                for b, (t0, tn) in enumerate(SBLOCKS):
                    dve.wait_ge(kk_sum, len(SBLOCKS) * hp + b + 1)
                    done(dve.tensor_scalar(kk[:, t0:t0 + tn], ps[:, b, 0:tn], 1e-12, None, ALU.max))
                for b, (t0, tn) in enumerate(SBLOCKS):
                    wait(b + 1)
                    dve.reciprocal(kk[:, t0:t0 + tn], kk[:, t0:t0 + tn]).then_inc(kk_inv, 1)
                dve.wait_ge(kk_rstd, len(SBLOCKS) * (hp + 1))
                done(dve.scalar_tensor_tensor(out=kk[:], in0=kf[:], scalar=par("k_k", hp), in1=kk[:], op0=ALU.mult,
                                              op1=ALU.mult))
                dve.wait_ge(za_evicted, NZ * (hp + 1))
                for d in range(2):
                    done(dve.tensor_scalar(bk[:, d, 1], bk[:, d, 0], par("k_a", hp), rest[:, bass.ds(hp, 1)], ALU.mult,
                                           ALU.add))
                wait()
                for d in range(2):
                    done(dve.tensor_tensor(bk[:, d, 1], bk[:, d, 1], kf[:, OFF[d]:OFF[d] + L], ALU.mult))
                for d in range(2):
                    done(dve.scalar_tensor_tensor(out=bk[:, d, 0], in0=kk[:, OFF[d]:OFF[d] + L], scalar=-1.0,
                                                  in1=bk[:, d, 0], op0=ALU.mult, op1=ALU.mult))
                wait()
                done(dve.tensor_tensor(e[:, 0:SEQ], bk[:, 0, 1, CTX:CTX + SEQ], bk[:, 1, 1, 0:SEQ], ALU.add))
                wait()
                dve.scalar_tensor_tensor(out=e[:, 0:SEQ], in0=e[:, 0:SEQ], scalar=par("r_k", hp), in1=r[:, CTX:TOK],
                                         op0=ALU.mult, op1=ALU.mult).then_inc(bonus_in, 1)
                for b in range(2):
                    dve.wait_ge(bonus_ps, 2 * hp + b + 1)
                    done(dve.tensor_tensor(out(hp, b), ps[:, b], v[:, CTX + b * BANK:CTX + (b + 1) * BANK], ALU.mult))
                for d in range(2):
                    done(dve.memset(e[:], 1.0))
                    wait()
                    done(dve.memset(e[:].rearrange("p (c t) -> p c t", t=CH)[:, :, END[1 - d]], 0.0))
                    wait()
                    walk = slice(None, None, (1, -1)[d])
                    done(dve.tensor_tensor_scan(ar[:, d, 1, walk], e[:, walk], ar[:, d, 0, walk], 0.0, ALU.mult, ALU.add))
                    wait()
                    cs = ar[:, d, 1].rearrange("p (c t) -> p c t", t=CH)
                    done(dve.tensor_copy(small[:, d, 0], cs[:, :, MID[d]]))
                    done(dve.tensor_copy(small[:, d, 1], cs[:, :, END[d]]))
                    wait()
                    done(dve.tensor_tensor(cs, cs, small[:, d, 0].unsqueeze(2).to_broadcast([P, NCH, CH]), ALU.subtract))
                    done(dve.tensor_tensor(small[:, d, 2], small[:, d, 1], small[:, d, 0], ALU.subtract))
                    wait()
                    here, there = ((slice(0, NCH - 1), slice(1, NCH)), (slice(1, NCH), slice(0, NCH - 1)))[d]
                    dve.tensor_tensor(small[:, d, 2, here], small[:, d, 2, here], small[:, d, 0, there],
                                      ALU.add).then_inc(log_ready, 1)
                    dve.tensor_tensor(ar[:, d, 0], ar[:, d, 1], ar[:, d, 0], ALU.subtract).then_inc(log_ready, 1)
                    dve.wait_ge(e_ready, 2 * hp + d + 1)
                    done(dve.tensor_tensor(bk[:, d], bk[:, d], e[:].unsqueeze(1).to_broadcast([P, 2, L]), ALU.mult))
                    dve.wait_ge(ar_ready, 2 * hp + d + 1)
                    done(dve.tensor_tensor(ar[:, d, 0], ar[:, d, 0], kk[:, OFF[d]:OFF[d] + L], ALU.mult))
                    done(dve.tensor_tensor(ar[:, d, 1], ar[:, d, 1], r[:, OFF[d]:OFF[d] + L], ALU.mult))
                    wait()
                for d in range(2):
                    done(dve.memset(sbd[:, d], 0.0))
                dve.wait_ge(vt_copied, 3 * (hp + 1))
                wait()
                dve.memset(kk[:], 0.0).then_inc(bulk_ready, 1)

                def masks(i, s):
                    rd = ROUNDS * hp + i
                    for d in range(2):
                        wait_apart(dve, go, tr_ready[s][d], rd)
                        dve.wait_ge(staged[s][d], 2 * rd + 1)
                        dve.tensor_scalar(bke[:, s, d], bk_s[:, s, d], small[:, d, 3, bass.ds(place(d, 2 * i + s), 1)],
                                          None, ALU.mult).then_inc(bke_ready[s][d], 1)
                    for q, dst in enumerate((ab, kr)):
                        for d in range(2):
                            wait_apart(dve, go, m_ready[s][d], 2 * rd + q + 1)
                            dve.copy_predicated(dst[:, s, d].rearrange("p h i t -> p (h i t)"),
                                                k.keep[:, d].rearrange("p h i t -> p (h i t)"),
                                                bank(s, d, q)).then_inc(masked[s][d], 1)
                        for d in range(2) if q == 0 else ():
                            dve.wait_ge(masked[s][d], 2 * rd + 1)
                            dve.tensor_tensor(atr[:, s, d], ab[:, s, d, :, 0],
                                              k.ident[:].unsqueeze(1).to_broadcast([P, 2, CH]),
                                              ALU.add).then_inc(at_ready[s][d], 1)

                def dve_round(i, last):
                    rd = ROUNDS * hp + i
                    for l in range(LEVELS):
                        for s, d in CHAINS:
                            dve.wait_ge(p_ready[s][d], LEVELS * rd + l + 1)
                            dve.tensor_tensor(pl[:, s, d, l % 2], half(s, d, P_HALF).rearrange("p (h t) -> p h t", h=2),
                                              k.level[:, d, l].unsqueeze(1).to_broadcast([P, 2, CH]),
                                              ALU.mult).then_inc(pl_ready[s][d], 1)
                        for s, d in CHAINS[:1]:
                            dve.wait_ge(t_ready[s][d], LEVELS * rd + l + 1)
                            dve.tensor_copy(*inverses(s, d, l)).then_inc(t_copied[s][d], 1)
                    for s, d in CHAINS:
                        dve.wait_ge(t_copied[s][d], LEVELS * (rd + 1))
                        dve.tensor_tensor(it[:, s, d], k.ident[:].unsqueeze(1).to_broadcast([P, 2, CH]),
                                          tb[:, s, d].bitcast(F32), ALU.subtract).then_inc(it_ready[s][d], 1)
                    for s, d in CHAINS:
                        dve.wait_ge(it_ready[s][d], rd + 1)
                        dve.wait_ge(g_ready[s][d], rd + 1)
                        dve.tensor_tensor(flat(er[:, s, d]), half(s, d, P_HALF), flat(it[:, s, d]),
                                          ALU.add).then_inc(er_ready[s][d], 1)
                    for s, d in CHAINS:
                        dve.wait_ge(n_ready[s][d], rd + 1)
                        dve.tensor_tensor(flat(ttf[:, s, d]), half(s, d, TT_HALF), flat(ttb[:, s, d]).bitcast(F32),
                                          ALU.add).then_inc(ttf_ready[s][d], 1)
                    for s in range(2):
                        step = NCH * hp + 2 * i + s
                        for d in range(2):
                            wait_apart(dve, go, st_ready[d], step + 1)
                            for h in range(2):
                                a, b = h * HD, (h + 1) * HD
                                dve.scalar_tensor_tensor(out=sbd[a:b, 1 - s, d, a:b], in0=sbd[a:b, s, d, a:b],
                                                         scalar=small[a:b, d, 3, bass.ds(place(d, 2 * i + s), 1)],
                                                         in1=half(s, d, S_HALF)[a:b, CH + a:CH + b], op0=ALU.mult,
                                                         op1=ALU.add).then_inc(st_done[d], 1)
                        for d in range(2):
                            wait_apart(dve, go, y_added[1 - d], step + d)
                            dve.wait_ge(y_ready[s][d], rd + 1)
                            yt = ytok[:, bass.ds(place(d, 2 * i + s, SC), 1)].squeeze(1)
                            dve.tensor_tensor(yt, yt, half(s, d, TT_HALF)[:, 0:CH], ALU.add).then_inc(y_added[d], 1)
                        if not last:
                            masks(i + 1, s)

                wait_apart(dve, masks_ready, bulk_ready, hp + 1)
                for s in range(2):
                    masks(0, s)
                with dve.Fori(0, ROUNDS - 1) as i:
                    dve_round(i, False)
                dve_round(ROUNDS - 1, True)

                G = 2 * SEQ // P
                y = kk[:, CTX:TOK].rearrange("p (g f) -> p g f", f=HD)
                for d in range(2):
                    dve.wait_ge(y_added[d], NCH * (hp + 1))
                done(dve.tensor_reduce(stat[:, 0], y, AX.X, ALU.add))
                wait()
                done(dve.tensor_scalar(stat[:, 1], stat[:, 0], 1.0 / HD, None, ALU.mult))
                wait()
                dve.tensor_tensor(y, y, stat[:, 1].unsqueeze(2).to_broadcast([P, G, HD]), ALU.subtract).then_inc(centred, 1)
                dve.wait_ge(gn_sq, hp + 1)
                done(dve.tensor_reduce(stat[:, 0], e[:, 0:SEQ].rearrange("p (g f) -> p g f", f=HD), AX.X, ALU.add))
                wait()
                done(dve.tensor_scalar(stat[:, 1], stat[:, 0], 1.0 / HD, GN_EPS, ALU.mult, ALU.add))
                wait()
                dve.reciprocal(stat[:, 2], stat[:, 1]).then_inc(gn_inv, 1)
                dve.wait_ge(gn_rstd, hp + 1)
                dve.tensor_tensor(y, y, stat[:, 3].unsqueeze(2).to_broadcast([P, G, HD]), ALU.mult).then_inc(normed, 1)
                for b in range(2):
                    dve.wait_ge(ln_done, 2 * hp + b + 1)
                    eb = e[:, b * BANK:(b + 1) * BANK]
                    done(dve.tensor_tensor(eb, eb, out(hp, b), ALU.add))
                    dve.wait_ge(gate_ps, 2 * hp + b + 1)
                    wait()
                    ins = dve.tensor_tensor(out(hp, b), eb, ps[:, 2 + b], ALU.mult)
                    if b == 0:
                        done(ins)
                ins.then_inc(pair_done, 1)
                assert c.n == DVE_PER_PAIR, c.n

        @block.tensor
        def _(pe):
            pe.wait_ge(go, 1)
            pe.wait_ge(lora_ready, 2)
            pe.wait_ge(zeroed, 6)
            pe.wait_ge(same_ready, 1)
            with pe.Fori(0, HP) as hp:
                pe.wait_ge(pair_done, hp)
                pe.wait_ge(hp_loaded, 128 * (hp + 1))
                for b, (t0, tn) in enumerate(SBLOCKS):
                    pe.wait_ge(sq_ready, len(SBLOCKS) * hp + b + 1)
                    pe.matmul(ps[:, b, 0:tn], k.same64[:], kk[:, t0:t0 + tn], start=True, stop=True).then_inc(kk_sum, 1)
                for i in range(NZ):
                    (d, b), q = divmod(i // 2, len(BLOCKS)), i % 2
                    t0, tn = BLOCKS[b]
                    pe.wait_ge(za_evicted, NZ * hp + max(i - 4, 0))
                    src = (tw, al)[q][:, OFF[d] + t0:OFF[d] + t0 + tn]
                    pe.matmul(ps[:, 3 + i % 5, 0:tn], (lw, la)[q][:, d], src, start=True, stop=True).then_inc(za_ready, 1)
                pe.wait_ge(za_evicted, NZ * (hp + 1))
                for b in range(3):
                    for j in range(4):
                        c = 4 * b + j
                        mm = pe.transpose(ps[:, 5 + b, j * CH:(j + 1) * CH], v[:, c * CH:(c + 1) * CH], k.ident[:])
                    mm.then_inc(vt_ready, 1)
                pe.wait_ge(bonus_in, hp + 1)
                for b in range(2):
                    pe.matmul(ps[:, b], k.same64[:], e[:, b * BANK:(b + 1) * BANK], start=True,
                              stop=True).then_inc(bonus_ps, 1)
                def products(i, s, d, first=False):
                    pe.wait_ge(staged[s][d], 2 * (ROUNDS * hp + i) + 1)
                    pe.wait_ge(arz_ready[s][d], 2 * (ROUNDS * hp + i + 1))
                    if not first:
                        pe.wait_ge(y_added[d], NCH * hp + 2 * i - 1 + s)
                    for q in range(2):
                        pe.matmul(bank(s, d, q), bk_s[:, s, d, q], arz[:, s, d].rearrange("p h i t -> p (h i t)"),
                                  start=True, stop=True).then_inc(m_ready[s][d], 1)

                def pe_round(i, last):
                    rd = ROUNDS * hp + i
                    for s, d in CHAINS:
                        pe.wait_ge(bke_ready[s][d], rd + 1)
                        pe.wait_ge(masked[s][d], 2 * (rd + 1))
                        for q in range(2):
                            mm = pe.transpose(half(s, d, S_HALF)[:, q * CH:(q + 1) * CH], bke[:, s, d, q], k.ident[:])
                        mm.then_inc(tr_ready[s][d], 1)
                    for l in range(LEVELS):
                        for s, d in CHAINS:
                            if l == 0:
                                pe.wait_ge(at_ready[s][d], rd + 1)
                                pe.wait_ge(tr_copied[s][d], rd + 1)
                            else:
                                pe.wait_ge(pl_ready[s][d], LEVELS * rd + l)
                                if l >= 2:
                                    pe.wait_ge(t_copied[s][d], LEVELS * rd + l)
                            for h in range(2):
                                t_inv = k.identr[:] if l == 0 else pl[:, s, d, 0, h] if l == 1 else tb[:, s, d, h]
                                mm = pe.matmul(half(s, d, P_HALF)[:, h * CH:(h + 1) * CH], atr[:, s, d, h], t_inv,
                                               start=True, stop=True)
                            mm.then_inc(p_ready[s][d], 1)
                        for s, d in CHAINS:
                            pe.wait_ge(pl_ready[s][d], LEVELS * rd + l + 1)
                            if l:
                                pe.wait_ge(t_copied[s][d], LEVELS * rd + l)
                            for h in range(2):
                                cols = slice(h * CH, (h + 1) * CH)
                                if l:
                                    pe.matmul(half(s, d, T_HALF)[:, cols], ttb[:, s, d, h], pl[:, s, d, l % 2, h],
                                              start=True, stop=True)
                                mm = pe.matmul(half(s, d, TT_HALF)[:, cols], pl[:, s, d, l % 2, h],
                                               ttb[:, s, d, h] if l else k.identr[:], start=True, stop=True)
                            mm.then_inc(t_ready[s][d], 1)
                    for s, d in CHAINS:
                        pe.wait_ge(t_copied[s][d], LEVELS * (rd + 1))
                        for h in range(2):
                            mm = pe.matmul(half(s, d, P_HALF)[:, h * CH:(h + 1) * CH], ab[:, s, d, h, 0],
                                           tb[:, s, d, h].bitcast(F32), start=True, stop=True)
                        mm.then_inc(g_ready[s][d], 1)

                    def add_kv(s):
                        step = NCH * hp + 2 * i + s
                        for d in range(2):
                            pe.wait_ge(staged[s][d], 2 * (rd + 1))
                            pe.wait_ge(er_ready[s][d], rd + 1)
                            pe.wait_ge(st_done[d], 2 * step)
                            for h in range(2):
                                a, b = h * HD, (h + 1) * HD
                                at = half(s, d, S_HALF)[:, a:b]
                                pe.matmul(at, ar_s[:, s, d, 0], sbd[:, s, d, a:b], start=True, stop=False)
                                mm = pe.matmul(at, kr[:, s, d, h, 0], vt(s, d)[:, a:b], start=False, stop=True)
                            mm.then_inc(w_ready[d], 1)

                    def vt(s, d):
                        return vtok[:, bass.ds(place(d, 2 * i + s, SC), 1)].squeeze(1)

                    for s, d in CHAINS:
                        pe.wait_ge(er_ready[s][d], rd + 1)
                        for h in range(2):
                            mm = pe.matmul(half(s, d, TT_HALF)[:, h * CH:(h + 1) * CH], er[:, s, d, h], ttb[:, s, d, h],
                                           start=True, stop=True)
                        mm.then_inc(n_ready[s][d], 1)
                    for s in range(2):
                        step = NCH * hp + 2 * i + s
                        add_kv(s)
                        if s and not last:
                            products(i + 1, 0, 0)
                        for d in range(2):
                            pe.wait_ge(ttf_ready[s][d], rd + 1)
                            pe.wait_ge(w_copied[d], step + 1)
                            for h in range(2):
                                a, b = h * HD, (h + 1) * HD
                                mm = pe.matmul(half(s, d, T_HALF)[:, a:b], ttf[:, s, d, h], wsb[:, d, a:b], start=True,
                                               stop=True)
                            mm.then_inc(u_ready[d], 1)
                        if s and not last:
                            products(i + 1, 0, 1)
                        for d in range(2):
                            pe.wait_ge(u_copied[d], step + 1)
                            at = half(s, d, S_HALF)[:, CH:2 * CH]
                            pe.matmul(at, bket[:, s, d, 0], usb[:, d], start=True, stop=False)
                            pe.matmul(at, bket[:, s, d, 1], vt(s, d), start=False, stop=True).then_inc(st_ready[d], 1)
                        for d in range(2):
                            for h in range(2):
                                a, b = h * HD, (h + 1) * HD
                                at = half(s, d, TT_HALF)[:, a:b]
                                pe.matmul(at, ar_s[:, s, d, 1], sbd[:, s, d, a:b], start=True, stop=False)
                                pe.matmul(at, ab[:, s, d, h, 1], usb[:, d, a:b], start=False, stop=False)
                                mm = pe.matmul(at, kr[:, s, d, h, 1], vt(s, d)[:, a:b], start=False, stop=True)
                            mm.then_inc(y_ready[s][d], 1)
                    for d in range(2) if not last else ():
                        products(i + 1, 1, d)

                pe.wait_ge(bulk_ready, hp + 1)
                for s, d in CHAINS:
                    products(0, s, d, first=True)
                with pe.Fori(0, ROUNDS - 1) as i:
                    pe_round(i, False)
                pe_round(ROUNDS - 1, True)
                pe.wait_ge(normed, hp + 1)
                for b in range(2):
                    for j in range(4):
                        c = CTX // CH + 4 * b + j
                        mm = pe.transpose(ps[:, b, j * CH:(j + 1) * CH], kk[:, c * CH:(c + 1) * CH], k.ident[:])
                    mm.then_inc(ln_ps, 1)
                for b in range(2):
                    pe.matmul(ps[:, 2 + b], gup[:], sgl[:, b * BANK:(b + 1) * BANK], start=True,
                              stop=True).then_inc(gate_ps, 1)




def merge(nc, k, hi, lo, d_w, d_gate):
    NB = SEQ // BANK
    ROUNDS = KT // 2
    U = 2 * NB
    gates = d_gate.rearrange("(h t) p n -> t p h n", h=2)
    parts = [k.o_na[:, t] for t in range(HP)] + [k.o_rw[:, t] for t in range(HP)]
    with Phase(nc, "mg") as ph:
        raw = ph.sb("w_raw", [P, 2, KT, P])
        wh, wl = ph.sb("w_hi", [P, 2, KT, P], F32R), ph.sb("w_lo", [P, 2, KT, P], F32R)
        oh = ph.sb("o_hi", [P, KT, SEQ], F32R)
        g = ph.sb("gates", [P, 2, 2, BANK])
        m = ph.sb("gated", [P, 2, BANK])
        whole = ph.sb("whole", [P, 2, BANK])
        ps = ph.psum(8)
        w_loaded = [ph.sem(f"w_loaded{s}") for s in range(2)]
        g_loaded = [ph.sem(f"g_loaded{s}") for s in range(2)]
        o_hi_done, o_lo_done, w_hi_done, w_lo_done, out_ready, gated, whole_ready, m_hi_done, m_lo_done = ph.sems(
            "o_hi_done o_lo_done w_hi_done w_lo_done out_ready gated whole_ready m_hi_done m_lo_done")
        block = ph.block()

        @block.sync
        def _(sp):
            with sp.Fori(0, ROUNDS) as i:
                for s in range(2):
                    sp.wait_ge(w_lo_done, 2 * i)
                    sp.dma_start(raw[:, s], d_w[2 * i + s]).then_inc(w_loaded[s], 16)
                for u in range(U):
                    s, b = divmod(u, NB)
                    sp.wait_ge(gated, 2 * (U * i + max(u - 1, 0)) if u else 2 * U * i)
                    sp.dma_start(g[:, u % 2], gates[2 * i + s][:, :, b * BANK:(b + 1) * BANK]).then_inc(g_loaded[u % 2], 16)

        @block.scalar
        def _(act):
            def split_w(i):
                for s in range(2):
                    act.wait_ge(out_ready, U * i)
                    act.wait_ge(w_loaded[s], 16 * (i + 1))
                    act.copy(wh[:, s], raw[:, s]).then_inc(w_hi_done, 1)

            split_w(0)
            for t in range(KT):
                act.copy(oh[:, t], parts[t]).then_inc(o_hi_done, 1)

            def act_round(i):
                for u in range(U):
                    s, b = divmod(u, NB)
                    wait_apart(act, o_hi_done, whole_ready, U * i + u + 1)
                    act.copy(hi[:, bass.ds(2 * i + s, 1), b * BANK:(b + 1) * BANK].squeeze(1),
                             whole[:, u % 2]).then_inc(m_hi_done, 1)

            with act.Fori(0, ROUNDS - 1) as i:
                act_round(i)
                split_w(i + 1)
            act_round(ROUNDS - 1)

        @block.vector
        def _(dve):
            def split_w(i):
                for s in range(2):
                    dve.wait_ge(w_hi_done, 2 * i + s + 1)
                    dve.tensor_tensor(wl[:, s], raw[:, s], wh[:, s].bitcast(F32), ALU.subtract).then_inc(w_lo_done, 1)

            split_w(0)
            for t in range(KT):
                dve.wait_ge(o_hi_done, t + 1)
                dve.tensor_tensor(parts[t].bitcast(F32R), parts[t], oh[:, t].bitcast(F32),
                                  ALU.subtract).then_inc(o_lo_done, 1)

            def split_lo(i, u):
                s, b = divmod(u, NB)
                at = (slice(None), bass.ds(2 * i + s, 1), slice(b * BANK, (b + 1) * BANK))
                dve.wait_ge(m_hi_done, U * i + u + 1)
                dve.tensor_tensor(lo[at].squeeze(1), whole[:, u % 2], hi[at].squeeze(1).bitcast(F32),
                                  ALU.subtract).then_inc(m_lo_done, 1)

            def dve_round(i):
                for u in range(U):
                    done = U * i + u
                    dve.wait_ge(out_ready, done + 1)
                    dve.wait_ge(g_loaded[u % 2], 16 * (NB * i + u // 2 + 1))
                    if u >= 2:
                        dve.wait_ge(m_lo_done, done - 1)
                    for h, dst in enumerate((m, whole)):
                        dve.tensor_tensor(dst[:, u % 2], ps[:, 2 * u + h], g[:, u % 2, h], ALU.mult).then_inc(gated, 1)
                    dve.wait_ge(gated, 2 * (done + 1))
                    dve.tensor_tensor(whole[:, u % 2], whole[:, u % 2], m[:, u % 2], ALU.add).then_inc(whole_ready, 1)
                    if u:
                        split_lo(i, u - 1)
                split_lo(i, U - 1)

            with dve.Fori(0, ROUNDS - 1) as i:
                dve_round(i)
                split_w(i + 1)
            dve_round(ROUNDS - 1)

        @block.tensor
        def _(pe):
            with pe.Fori(0, ROUNDS) as i:
                for u in range(U):
                    s, b = divmod(u, NB)
                    pe.wait_ge(w_lo_done, 2 * i + s + 1)
                    pe.wait_ge(gated, 2 * U * i)
                    for h in range(2):
                        for kt in range(HP * h, HP * (h + 1)):
                            tok = slice(b * BANK, (b + 1) * BANK)
                            if u == 0:
                                pe.wait_ge(o_lo_done, kt + 1)
                            mm = three(pe, ps[:, 2 * u + h], wh[:, s, kt], wl[:, s, kt], oh[:, kt, tok],
                                       parts[kt].bitcast(F32R)[:, tok], kt == HP * h, kt == HP * (h + 1) - 1)
                    mm.then_inc(out_ready, 1)


def hybrid_layer(nc, par, x, ctx, w_ada, w_ffn1, w_ffn2, w_q, w_k, w_v, w_rw, w_gate, rpb, w_up, a_up, g_up,
                 w_merge, w_out, out):
    k = Kept()
    k.d_par, k.d_x, k.d_ctx, k.d_w_ada = par, x, ctx, w_ada
    d_q = nc.dram_tensor("q_scratch", (HP, P, SEQ), F32).ap()
    d_k = nc.dram_tensor("k_scratch", (HP, P, TOK), F32).ap()
    d_v = nc.dram_tensor("v_scratch", (TOK // P, P, HEADS * HD), F32).ap()
    d_rw = nc.dram_tensor("rw_scratch", (RW_TILES, P, STREAM), F32).ap()
    k.d_x_kept = nc.dram_tensor("x_scratch", (P, KT, SEQ), F32).ap()
    d_gate = nc.dram_tensor("gate_scratch", (2 * KT, P, SEQ), F32).ap()
    table = (2 * WIN_H + 1) * RPB_ROW
    k.d_rpb_source = bass.AP(tensor=rpb.tensor, offset=0, ap=[[table, HEADS], [0, GRID_W], [1, table]])
    k.d_rpb_copies = nc.dram_tensor("rpb_scratch", (HEADS, GRID_W, table), F32).ap()
    d_rpb = bass.AP(tensor=k.d_rpb_copies.tensor, offset=GRID_W - 1,
                    ap=[[GRID_W * table, HEADS], [table - 1, GRID_W], [RPB_ROW, 2 * WIN_H + 1], [1, GRID_W]])

    def sb(stack, name, shape, dtype=F32):
        return stack.enter_context(nc.sbuf_tensor(name, shape, dtype))

    with ExitStack() as whole:
        k.par = sb(whole, "params", [P, PAR_COLS])
        k.ones = sb(whole, "ones", [P, P])
        k.ident, k.identr = sb(whole, "ident", [P, P]), sb(whole, "ident_r", [P, P], F32R)
        k.mod = sb(whole, "mod", [P, NMOD * KT, 2])
        k.gain, k.gate = sb(whole, "gain", [P, 3, 2, KT]), sb(whole, "gate", [P, 3, 2, KT])

        with ExitStack() as front:
            k.x = sb(front, "x_front", [P, KT, SEQ])
            k.ctx = sb(front, "context", [P, KT, CTX])
            load_constants(nc, k)
            modulation(nc, k)
            hi, lo = sb(front, "h_hi", [P, KT, SEQ], F32R), sb(front, "h_lo", [P, KT, SEQ], F32R)
            norm(nc, k, "norm1", k.x, SEQ, 0, 0, hi, lo)
            swiglu(nc, k, "ffn1", k.x, SEQ, 0, 0, hi, lo, w_ffn1)
            norm(nc, k, "norm1c", k.ctx, CTX, 0, 1, hi, lo)
            swiglu(nc, k, "ffn1c", k.ctx, CTX, 0, 1, hi, lo, w_ffn1)

            hic, loc = sb(front, "hc_hi", [P, KT, CTX], F32R), sb(front, "hc_lo", [P, KT, CTX], F32R)
            norm(nc, k, "norm2", k.x, SEQ, 1, 0, hi, lo)
            norm(nc, k, "norm2c", k.ctx, CTX, 1, 1, hic, loc)
            latents = [(hi[:, :, a:a + n], lo[:, :, a:a + n], n) for a, n in halves(SEQ)]
            both = latents + [(hic[:], loc[:], CTX)]
            project(nc, k, "pk", HP, w_k, both, "scale", d_k, 1.0)
            project(nc, k, "prw", RW_TILES, w_rw, both, "shift", d_rw)
            project(nc, k, "pq", HP, w_q, latents, "scale", d_q, HD ** -0.5)
            project(nc, k, "pg", 2 * KT, w_gate, latents, "gate", d_gate, PAR["b_gate"][0])
            project_v(nc, k, hi, lo, hic, loc, w_v, d_v)

        k.o_rw = sb(whole, "o_rw", [P, HP, SEQ])
        with ExitStack() as masks:
            k.same64 = sb(masks, "same_head", [P, P])
            k.keep = sb(masks, "keep", [P, 2, 2, 2, CH], U8)
            k.level = sb(masks, "level", [P, 2, LEVELS, CH])
            rwkv(nc, k, d_rw, w_up, a_up, g_up)
        k.x = sb(whole, "x", [P, KT, SEQ])
        with ExitStack() as mix:
            k.o_na = sb(mix, "o_na", [P, HP, SEQ])
            attention(nc, k, d_q, d_k, d_v, d_rpb)
            hi, lo = sb(mix, "m_hi", [P, KT, SEQ], F32R), sb(mix, "m_lo", [P, KT, SEQ], F32R)
            merge(nc, k, hi, lo, w_merge, d_gate)
            merged = [(hi[:, :, a:a + n], lo[:, :, a:a + n], n) for a, n in halves(SEQ)]
            project(nc, k, "po", KT, w_out, merged, "residual")

        with ExitStack() as back:
            hi, lo = sb(back, "h2_hi", [P, KT, SEQ], F32R), sb(back, "h2_lo", [P, KT, SEQ], F32R)
            norm(nc, k, "norm3", k.x, SEQ, 2, 0, hi, lo)
            swiglu(nc, k, "ffn2", k.x, SEQ, 2, 0, hi, lo, w_ffn2)
            norm(nc, k, "norm4", k.x, SEQ, d_out=out)


def pieces(w):
    rows, cols = w.shape
    return w.reshape(rows // P, P, cols // P, P).transpose(2, 1, 0, 3)


def ffn_pieces(wg, wu, wd):
    g, u = pieces(wg), pieces(wu)
    d = wd.reshape(FT, P, KT, P)
    return np.stack([g[0::2], u[0::2], g[1::2], u[1::2], d[0::2], d[1::2]], 1).reshape(3 * FT, P, KT, P)


def feature_tiles(a):
    return a.T.reshape(-1, P, a.shape[0]).transpose(1, 0, 2)


def layout(a):
    w, mu = a["w_in"][0], a["rw_mu"][0]
    NA, RW = HEADS * HD, RW_TILES * P
    vectors = [a["c"], a["c_ctx"], a["b_ada"], a["norm_ffn1"], a["norm_mix"], a["norm_ffn2"], a["norm_final"],
               a["b_gate"], mu[0], mu[1], a["rw_w0"], a["rw_a0"], a["rw_k_k"], a["rw_k_a"], a["rw_r_k"],
               a["rw_ln_w"], a["rw_ln_b"]]
    rpb = np.zeros((HEADS, 2 * WIN_H + 1, RPB_ROW), np.float32)
    left = GRID_W - WIN_W
    rpb[:, 1:2 * WIN_H, left:left + 2 * WIN_W - 1] = a["na_rpb"][0]
    return {
        "par": np.concatenate([v.reshape(-1, P).T for v in vectors], 1),
        "x": feature_tiles(a["x"][0]),
        "ctx": feature_tiles(a["ctx"][0]),
        "w_ada": a["w_ada"][0].reshape(KT, P, NMOD * D // BANK, BANK).transpose(2, 1, 0, 3),
        "w_ffn1": ffn_pieces(a["ffn1_wg"][0], a["ffn1_wu"][0], a["ffn1_wd"][0]),
        "w_ffn2": ffn_pieces(a["ffn2_wg"][0], a["ffn2_wu"][0], a["ffn2_wd"][0]),
        "w_q": pieces(w[:, 0:NA]),
        "w_k": pieces(w[:, NA:2 * NA]),
        "w_v": w[:, 2 * NA:3 * NA].reshape(KT, P, NA).transpose(1, 0, 2),
        "w_rw": pieces(w[:, 3 * NA:3 * NA + RW]),
        "w_gate": pieces(w[:, 3 * NA + RW:]),
        "rpb": rpb,
        "w_up": a["rw_w_up"][0],
        "a_up": a["rw_a_up"][0],
        "g_up": a["rw_g_up"][0],
        "w_merge": pieces(np.concatenate([a["p_na"][0], a["p_rw"][0]])),
        "w_out": pieces(a["w_out"][0]),
    }


def kernel(**inputs):
    import concourse.bacc as _bacc
    from concourse.bass_utils import run_bass_kernel_spmd as _run

    nc = _bacc.Bacc("TRN2", target_bir_lowering=False, num_devices=1)
    arrays, args = {}, {}
    for name, a in layout({name: np.asarray(a) for name, a in inputs.items()}).items():
        a = np.ascontiguousarray(a)
        arrays[f"in_{name}_dram"] = a
        args[name] = nc.dram_tensor(f"in_{name}_dram", a.shape, F32, kind="ExternalInput").ap()
    out = nc.dram_tensor("out_0_dram", (P, KT, SEQ), F32, kind="ExternalOutput").ap()
    hybrid_layer(nc, out=out, **args)
    r = _run(nc, [arrays], core_ids=[0])
    return r.results[0]["out_0_dram"].transpose(2, 1, 0).reshape(1, SEQ, D)
```
